# Optimizing a Trainium2 kernel written in Bass

```python
import math
import jax
import jax.numpy as jnp
from jax import lax
import numpy as np

D_MODEL = 1024
BATCH = 1
SEQ = 2048
DEPTH = 1

CHUNK = 64
MIX_WIDTH = D_MODEL
ATT_WIDTH = MIX_WIDTH // 2
N_ATT_HEADS = 8
ATT_HEAD_DIM = ATT_WIDTH // N_ATT_HEADS
KV_LATENT = 128
N_IDX_HEADS = 8
IDX_HEAD_DIM = 64
TOPK_MAX = 256
Q_BLOCK = 128
POOL_WIDTH = MIX_WIDTH - ATT_WIDTH
POOL_WINDOWS = (2, 4, 8, 16)
N_POOL_GROUPS = len(POOL_WINDOWS)
POOL_GROUP = POOL_WIDTH // N_POOL_GROUPS
D_FF = 2816
CONV_WIDTH = 3
EPS = 1e-6

COL_Q = N_ATT_HEADS * ATT_HEAD_DIM
COL_C = KV_LATENT
COL_QI = N_IDX_HEADS * IDX_HEAD_DIM
COL_KI = IDX_HEAD_DIM
COL_WI = N_IDX_HEADS
COL_U = POOL_WIDTH
SPLITS = tuple(np.cumsum([COL_Q, COL_C, COL_QI, COL_KI, COL_WI]).tolist())
IN_COLS = COL_Q + COL_C + COL_QI + COL_KI + COL_WI + COL_U

kernel_name = "hybrid_dsa_pool_convffn"

def rmsnorm(x, g):
    xf = x.astype(jnp.float32)
    y = xf * lax.rsqrt(jnp.mean(xf * xf, axis=-1, keepdims=True) + EPS)
    return (y * g.astype(jnp.float32)).astype(x.dtype)

def alibi_slopes(n_heads):
    h = jnp.arange(1, n_heads + 1, dtype=jnp.float32)
    return jnp.exp2(-8.0 * h / n_heads)

def dsa_attention(q, c, q_idx, k_idx, w_idx, w_uk, w_uv):
    B, S, H, dh = q.shape
    n_top = min(TOPK_MAX, S // 4)
    nb = S // Q_BLOCK
    scale = ATT_HEAD_DIM ** -0.5
    w_idx = w_idx * (N_IDX_HEADS ** -0.5) * (IDX_HEAD_DIM ** -0.5)
    q_lat = jnp.einsum("bshd,hdc->bshc", q, w_uk)
    slopes = alibi_slopes(H)
    key_chunk = jnp.arange(S, dtype=jnp.int32) // CHUNK
    qpos_blocks = jnp.arange(S, dtype=jnp.int32).reshape(nb, Q_BLOCK)

    def to_blocks(a):
        return a.reshape((B, nb, Q_BLOCK) + a.shape[2:]).swapaxes(0, 1)

    def block(args):
        ql, qi, wi, qpos = args
        rel = jax.nn.relu(jnp.einsum("bqid,bsd->bqis", qi, k_idx).astype(jnp.float32))
        score = jnp.einsum("bqi,bqis->bqs", wi.astype(jnp.float32), rel)
        admissible = key_chunk[None, :] <= (qpos // CHUNK)[:, None]
        score = jnp.where(admissible[None], score, -jnp.inf)
        vals, idx = lax.top_k(score, n_top)
        valid = jnp.isfinite(vals)
        c_sel = jax.vmap(lambda cb, ib: cb[ib])(c, idx)
        logits = jnp.einsum("bqhc,bqkc->bqhk", ql, c_sel).astype(jnp.float32) * scale
        dist = jnp.abs(qpos[None, :, None] - idx).astype(jnp.float32)
        logits = logits - slopes[None, None, :, None] * dist[:, :, None, :]
        logits = jnp.where(valid[:, :, None, :], logits, -jnp.inf)
        p = jax.nn.softmax(logits, axis=-1).astype(c.dtype)
        return jnp.einsum("bqhk,bqkc->bqhc", p, c_sel)

    o_lat = lax.map(block, (to_blocks(q_lat), to_blocks(q_idx), to_blocks(w_idx), qpos_blocks))
    o_lat = o_lat.swapaxes(0, 1).reshape(B, S, H, KV_LATENT)
    o = jnp.einsum("bshc,hcd->bshd", o_lat, w_uv)
    return o.reshape(B, S, H * dh)

def multiscale_pool(u, w_pool, pool_scale):
    B, S, W = u.shape
    uf = u.astype(jnp.float32)
    cs = jnp.concatenate([jnp.zeros((B, 1, W), jnp.float32), jnp.cumsum(uf, axis=1)], axis=1)
    t = jnp.arange(S, dtype=jnp.int32)
    outs = []
    for g, win in enumerate(POOL_WINDOWS):
        sl = slice(g * POOL_GROUP, (g + 1) * POOL_GROUP)
        start = jnp.maximum(t + 1 - win, 0)
        win_sum = cs[:, t + 1, sl] - cs[:, start, sl]
        count = (t + 1 - start).astype(jnp.float32)
        outs.append(win_sum / count[None, :, None] - uf[:, :, sl])
    pooled = jnp.stack(outs, axis=2)
    mixed = jnp.einsum("bsgc,gcd->bsgd", pooled, w_pool.astype(jnp.float32)).reshape(B, S, W)
    return (mixed * pool_scale.astype(jnp.float32)).astype(u.dtype)

def conv_glu_ffn(h, w_up, conv_w, conv_b, w_down):
    S = h.shape[1]
    a = h @ w_up
    ap = jnp.pad(a, ((0, 0), (CONV_WIDTH - 1, 0), (0, 0)))
    conv = conv_b + sum(ap[:, j:j + S] * conv_w[j] for j in range(CONV_WIDTH))
    gate, up = jnp.split(conv, 2, axis=-1)
    return (jax.nn.silu(gate) * up) @ w_down

def setup_inputs(seed: int = 0) -> dict:
    key = jax.random.key(seed)
    ks = jax.random.split(key, 16)
    L = DEPTH
    f32 = jnp.float32
    nrm = lambda k, shape, s: jax.random.normal(k, shape, f32) * s
    return {
        "x": jax.random.normal(ks[0], (BATCH, SEQ, D_MODEL), f32),
        "g_mix": 1.0 + nrm(ks[1], (L, D_MODEL), 0.01),
        "w_in": nrm(ks[2], (L, D_MODEL, IN_COLS), D_MODEL ** -0.5),
        "g_kv": 1.0 + nrm(ks[3], (L, KV_LATENT), 0.01),
        "w_uk": nrm(ks[4], (L, N_ATT_HEADS, ATT_HEAD_DIM, KV_LATENT), ATT_HEAD_DIM ** -0.5),
        "w_uv": nrm(ks[5], (L, N_ATT_HEADS, KV_LATENT, ATT_HEAD_DIM), KV_LATENT ** -0.5),
        "w_pool": nrm(ks[6], (L, N_POOL_GROUPS, POOL_GROUP, POOL_GROUP), POOL_GROUP ** -0.5),
        "pool_scale": 1.0 + nrm(ks[7], (L, POOL_WIDTH), 0.1),
        "w_o": nrm(ks[8], (L, MIX_WIDTH, D_MODEL), MIX_WIDTH ** -0.5),
        "g_ffn": 1.0 + nrm(ks[9], (L, D_MODEL), 0.01),
        "w_up": nrm(ks[10], (L, D_MODEL, 2 * D_FF), D_MODEL ** -0.5),
        "conv_w": nrm(ks[11], (L, CONV_WIDTH, 2 * D_FF), CONV_WIDTH ** -0.5),
        "conv_b": nrm(ks[12], (L, 2 * D_FF), 0.01),
        "w_down": nrm(ks[13], (L, D_FF, D_MODEL), D_FF ** -0.5),
        "g_final": 1.0 + nrm(ks[14], (D_MODEL,), 0.01),
    }

def reference(x, g_mix, w_in, g_kv, w_uk, w_uv, w_pool, pool_scale, w_o,
              g_ffn, w_up, conv_w, conv_b, w_down, g_final):
    B, S, _ = x.shape
    for l in range(DEPTH):
        h = rmsnorm(x, g_mix[l])
        proj = h @ w_in[l]
        q, c_raw, q_idx, k_idx, w_idx, u_pool = jnp.split(proj, SPLITS, axis=-1)
        q = q.reshape(B, S, N_ATT_HEADS, ATT_HEAD_DIM)
        c = rmsnorm(c_raw, g_kv[l])
        q_idx = q_idx.reshape(B, S, N_IDX_HEADS, IDX_HEAD_DIM)
        a_out = dsa_attention(q, c, q_idx, k_idx, w_idx, w_uk[l], w_uv[l])
        b_out = multiscale_pool(u_pool, w_pool[l], pool_scale[l])
        x = x + jnp.concatenate([a_out, b_out], axis=-1) @ w_o[l]
        x = x + conv_glu_ffn(rmsnorm(x, g_ffn[l]), w_up[l], conv_w[l], conv_b[l], w_down[l])
    return rmsnorm(x, g_final)


_drawn_inputs = setup_inputs


def setup_inputs(seed=0):
    import zlib

    import numpy as np

    out = dict(_drawn_inputs(seed))
    spreads = {}
    factors = {'g_kv': 8.0, 'g_ffn': 32.097, 'conv_b': 32.543, 'g_final': 32.935, 'pool_scale': 3.363}
    for name, (base, spread) in spreads.items():
        noise = np.random.default_rng([zlib.crc32(name.encode()), seed]).standard_normal(out[name].shape)
        drawn = base * np.exp(spread * noise) if base else spread * noise
        out[name] = jnp.asarray(drawn.astype(out[name].dtype))
    for name, factor in factors.items():
        out[name] = (out[name] * factor).astype(out[name].dtype)
    return out
```

```python
import concourse.bass as bass
from concourse import mybir
from contextlib import ExitStack

F32 = mybir.dt.float32
F32R = mybir.dt.float32r
BF16 = mybir.dt.bfloat16
U32 = mybir.dt.uint32
U8 = mybir.dt.uint8
I32 = mybir.dt.int32
I16 = mybir.dt.int16
ALU = mybir.AluOpType
ACT = mybir.ActivationFunctionType

P = 128
SEQ = 2048
DM = 1024
KT = DM // P
TB = 512
NBLK = SEQ // TB
JT = TB // P
NT = SEQ // P
H = 8
DH = 64
CL = 128
TOPK = 256
FF = 2816
NF = FF // P
FF_PARTS = [(0, 8), (8, 15), (15, NF)]
PART = max(b - a for a, b in FF_PARTS)
COL_Q, COL_C, COL_QI, COL_KI, COL_U = 0, 512, 640, 1152, 1224
KW = 72
WINDOWS = (2, 4, 8, 16)
HALO = 16
CHUNK = 1024
CONV = 3
EPS = 1e-6
BIG = 1e30
FLT_MAX = 3.4028234663852886e38
DIST_BASE = SEQ - P
NRING = 2
NLG = 4


def weight_units(w):
    def cols(name, a, n, k0=0, k1=KT):
        if name == "w_in":
            src = w[name][:, KT * a:KT * (a + n)].rearrange("p (k n) -> p k n", n=n)
        else:
            src = w[name][a // P]
        return src[:, k0:k1, :], k1 - k0, n

    def ffn():
        out = []
        for a, b in FF_PARTS:
            for i in range(a, b):
                out += [cols("w_up", i * P, P), cols("w_up", FF + i * P, P)]
            out += [cols("w_down", m * P, P, a, b) for m in range(KT)]
        return out

    units, at = [], {}
    for g in range(NBLK):
        at["in", g] = len(units)
        units += [cols("w_in", COL_C, CL), cols("w_in", COL_KI, KW)]
        for start in (COL_U, COL_QI, COL_Q):
            units += [cols("w_in", start + m * P, P) for m in range(4)]
        if g:
            at["ffn", g - 1] = len(units)
            units += ffn()
        at["o", g] = len(units)
        units += [cols("w_o", m * P, P) for m in range(KT)]
    at["ffn", NBLK - 1] = len(units)
    units += ffn()
    return units, at


def program(nc, x, y, w, g_mix, g_kv, w_uk, w_uv, w_pool, pool_scale, g_ffn, conv_w, conv_b, g_final):
    units, unit_at = weight_units(w)
    NU = len(units)

    ctx = ExitStack()
    with ctx:
        def sb(name, shape, dt, stack=None):
            return (stack or ctx).enter_context(nc.sbuf_tensor(name, shape, dt))

        def sem(name):
            return ctx.enter_context(nc.semaphore(name))

        wraw = sb("wraw", [P, NRING, KT, P], F32)
        wH, wL = sb("wH", [P, NRING, KT, P], F32R), sb("wL", [P, NRING, KT, P], F32R)
        ident = sb("ident", [P, P], F32)
        ones = sb("ones", [P, P], F32)
        dist = sb("dist", [P, SEQ], I16)
        ukH, ukL = sb("ukH", [P, H, CL], F32R), sb("ukL", [P, H, CL], F32R)
        uvH, uvL = sb("uvH", [P, H * DH], F32R), sb("uvL", [P, H * DH], F32R)
        wpH, wpL = sb("wpH", [P, 4, P], F32R), sb("wpL", [P, 4, P], F32R)
        gm, gf = sb("gm", [P, KT], F32), sb("gf", [P, KT], F32)
        psc = sb("psc", [P, 4], F32)
        gkv = sb("gkv", [P, CL], F32)
        cw = sb("cw", [P, 3, 2 * NF], F32)
        cb = sb("cb", [P, 2 * NF], F32)
        ahalo = sb("ahalo", [P, 2, 2 * NF, 2], F32)
        uhalo = sb("uhalo", [P, 4, HALO], F32)
        invc = sb("invc", [P, 4, HALO], F32)
        st = sb("st", [P, 24], F32)
        wabs, wsgn, wS = sb("wabs", [P, JT, H], F32), sb("wsgn", [P, JT, H], F32), sb("wS", [P, JT, H], F32)
        cand, drop, cnt = sb("cand", [P, 4], U32), sb("drop", [P, 4], U32), sb("cnt", [P, 4], F32)
        need = sb("need", [P, 2], F32)
        mx, nb = sb("mx", [P, 4, NBLK], F32), sb("nb", [P, 4], F32)
        lsum, rl = sb("lsum", [P, 2, 4, NBLK], F32), sb("rl", [P, 4], F32)

        def area(*layouts):
            made = []
            for layout in layouts:
                with ExitStack() as s:
                    made.append([sb(n, shape, dt, s) for n, shape, dt in layout])
            return made

        (kiH, kiL, cTH, cTL, cH, cL), (gH, gL, asb, acc, th), (xn2,), (yb,), (distI, distN, distF) = area(
            [("kiH", [P, SEQ], F32R), ("kiL", [P, SEQ], F32R), ("cTH", [P, SEQ], F32R), ("cTL", [P, SEQ], F32R),
             ("cH", [P, NT, CL], F32R), ("cL", [P, NT, CL], F32R)],
            [("gH", [P, PART, TB], F32R), ("gL", [P, PART, TB], F32R), ("asb", [P, 2, TB + 2], F32),
             ("acc", [P, 2, 2, TB], F32), ("th", [P, TB], F32)],
            [("xn2", [P, JT, DM], F32)],
            [("yb", [P, JT, DM], F32)],
            [("distI", [P, SEQ], I32), ("distN", [P, SEQ], F32), ("distF", [P, SEQ], F32)])
        sb("key_area", [P, 6 * SEQ], F32)
        actH, actL = sb("actH", [P, KT, TB], F32R), sb("actL", [P, KT, TB], F32R)
        (xb,), (qiS,), (prob,) = area(
            [("xb", [P, JT, DM], F32)], [("qiS", [P, H, TB], F32R)], [("prob", [P, 2, SEQ], F32)])
        sb("residual_area", [P, JT * DM], F32)
        (score,), (xa, xn), (uT, s0, s1, pH, pL) = area(
            [("score", [P, JT, SEQ], F32)],
            [("xa", [P, JT, DM], F32), ("xn", [P, JT, DM], F32)],
            [("uT", [P, 4, HALO + TB], F32), ("s0", [P, HALO + TB], F32), ("s1", [P, HALO + TB], F32),
             ("pH", [P, 4, TB], F32R), ("pL", [P, 4, TB], F32R)])
        sb("score_area", [P, JT * SEQ], F32)
        (qlH0, qlL0, qlH1, qlL1, pt, dgR, oH, oL), (poolF, qF, cF, cS, kwS), (_, counted, stage), (_, eqm, tiem, rank, gfin), \
            (ukR, ukS, uvS, wpS) = area(
            [("qlH0", [P, H, P], F32R), ("qlL0", [P, H, P], F32R), ("qlH1", [P, H, P], F32R), ("qlL1", [P, H, P], F32R),
             ("pt", [P, 2, 2, TB], F32R), ("dgR", [P, 4, P], F32), ("oH", [P, 4, P], F32R), ("oL", [P, 4, P], F32R)],
            [("poolF", [P, 4, TB], F32), ("qF", [P, 4, TB], F32), ("cF", [P, JT, CL], F32), ("cS", [P, TB], F32),
             ("kwS", [KW, TB], F32)],
            [("gap", [P, 8 * TB], F32), ("counted", [P, JT, SEQ], U8), ("stage", [P, 2, TB], F32)],
            [("gap2", [P, 8 * TB], F32), ("eqm", [P, SEQ], U8), ("tiem", [P, SEQ], U8), ("rank", [P, SEQ], I16),
             ("gfin", [P, DM], F32)],
            [("ukR", [P, 4, CL], F32), ("ukS", [P, H, CL], F32), ("uvS", [P, H * DH], F32), ("wpS", [P, 4, P], F32)])
        qlH, qlL = (qlH0, qlH1), (qlL0, qlL1)

        key_tiles = [kiH, kiL, cTH, cTL, cH, cL]
        key_store = [nc.dram_tensor(f"key_store{i}", [NBLK, P, TB], F32, kind="Internal").ap() for i in range(6)]
        x1_store = nc.dram_tensor("x1_store", [SEQ, DM], F32, kind="Internal").ap()

        def key_columns(i, b0, b1):
            t = f(key_tiles[i][:])
            t = t if i < 4 else t.rearrange("p t c -> p (t c)")
            return t[:, b0 * TB:b1 * TB].rearrange("p (b n) -> p b n", n=TB)

        ps = ctx.enter_context(nc.psum_tensor("ps", [P, 8, 512], F32))

        c_loaded = sem("c_loaded")
        c_made = sem("c_made")
        c_hi, c_lo, uk_scaled = sem("c_hi"), sem("c_lo"), sem("uk_scaled")
        w_loaded = [sem(f"w_loaded{i}") for i in range(NRING)]
        w_hi, w_lo, unit_done = sem("w_hi"), sem("w_lo"), sem("unit_done")
        x_loaded = [sem(f"x_loaded{j}") for j in range(JT)]
        gfin_loaded = sem("gfin_loaded")
        sq_done, var_ready, std_ready, xn_ready = sem("sq_done"), sem("var_ready"), sem("std_ready"), sem("xn_ready")
        csq_done = sem("csq_done")
        tr_full, tr_hi, tr_free = sem("tr_full"), sem("tr_hi"), sem("tr_free")
        pooled_full, pj_act, pj_dve, pj_hi = sem("pooled_full"), sem("pj_act"), sem("pj_dve"), sem("pj_hi")
        lg_full, lg_free, relu_done = sem("lg_full"), sem("lg_free"), sem("relu_done")
        lq_full, ttr_done, sums_copied = sem("lq_full"), sem("ttr_done"), sem("sums_copied")
        tok_ready, cF_hi = sem("tok_ready"), sem("cF_hi")
        pool_ready = sem("pool_ready")
        q_hi, q_lo = sem("q_hi"), sem("q_lo")
        d_ready = sem("d_ready")
        nb_ready, exp_done, pv_done = sem("nb_ready"), sem("exp_done"), sem("pv_done")
        o_free, dg_ready, o_hi, o_lo = sem("o_free"), sem("dg_ready"), sem("o_hi"), sem("o_lo")
        st_ready = sem("st_ready")
        conv_in, taps_done, tanh_done, gu_ready, g_hi, g_lo = (sem("conv_in"), sem("taps_done"), sem("tanh_done"),
                                                              sem("gu_ready"), sem("g_hi"), sem("g_lo"))
        kv_made, kv_saved, kv_loaded, ki_loaded = sem("kv_made"), sem("kv_saved"), sem("kv_loaded"), sem("ki_loaded")
        x1_saved = sem("x1_saved")
        xr_loaded = [sem(f"xr_loaded{j}") for j in range(JT)]
        x1_loaded = [sem(f"x1_loaded{j}") for j in range(JT)]
        x1_ready, y_ready, y_stored = sem("x1_ready"), sem("y_ready"), sem("y_stored")
        dve_step, act_step, pool_step = sem("dve_step"), sem("act_step"), sem("pool_step")

        def f(ap):
            return ap.bitcast(F32)

        def keys(t):
            return P * (t + 1)

        def chunks(t):
            return [(a, min(CHUNK, keys(t) - a)) for a in range(0, keys(t), CHUNK)]

        def quad(g, n, q):
            return 4 * q, min(4, JT * g + n // H + 1 - 4 * q)

        def prob_slots(g):
            slots = 2 * SEQ // (TB * (g + 1))
            return slots, min(3, slots - 1)

        def value_steps(g):
            Q, (_, ahead) = g + 1, prob_slots(g)
            NH = JT * H
            steps = [("query", 0)] + [("logits", n, q) for n in range(ahead) for q in range(Q)]
            last = None
            for n in range(NH):
                for q in range(Q):
                    m = n + ahead
                    if q == 0 and (m + 1) % H == 0 and m + 1 < NH:
                        steps.append(("query", (m + 1) // H))
                    if m < NH:
                        steps.append(("logits", m, q))
                    steps.append(("turn", n, q))
                    if last:
                        steps.append(("value",) + last)
                    last = (n, q)
                    if q == 0 and n % 4 == 0 and n:
                        steps.append(("recip", n // 4 - 1))
                    if q == 0 and n % 4 == 1 and n > 4:
                        steps.append(("norm", n // 4 - 1))
                if n % 4 == 0 and n:
                    steps.append(("sums", n // 4 - 1))
                if n % 4 == 1 and n > 4:
                    steps.append(("out", n // 4 - 1))
            steps += [("value",) + last] + [(k, NH // 4 - 1) for k in ("recip", "sums", "norm", "out")]
            return steps

        def sums_after_o(g):
            return KT * (g + 1) + KT * len(FF_PARTS) * g

        def sums_after_ffn(b):
            return KT * (b + 1) + KT * len(FF_PARTS) * (b + 1)

        def o_banks(G):
            b = 2 if G % 2 == 0 else 6
            return ps[:, b:b + 2, :].rearrange("p b (h s n) -> p (b h) s n", h=2, s=2)

        def lg(k, n):
            b = 2 * (k % NLG)
            return ps[:, b:b + 2, :].rearrange("p b n -> p (b n)")[:, 0:n]

        def prob_row(g, n):
            slots, _ = prob_slots(g)
            w = TB * (g + 1)
            return prob[:].rearrange("p a b -> p (a b)")[:, (n % slots) * w:(n % slots + 1) * w]

        class Count:
            def __init__(self):
                self.n = 0

            def up(self, k=1):
                self.n += k
                return self.n

        len_ffn = 2 * NF + KT * len(FF_PARTS)
        block = ctx.enter_context(nc.Block())
        NCONST = 9

        @block.sync
        def _(sp):
            sp.dma_start(gm[:], g_mix).then_inc(c_loaded, 16)
            sp.dma_start(gf[:], g_ffn).then_inc(c_loaded, 16)
            sp.dma_start(psc[:], pool_scale).then_inc(c_loaded, 16)
            sp.dma_start(gkv[:], g_kv.rearrange("(a n) -> a n", a=1).to_broadcast([P, CL])).then_inc(c_loaded, 16)
            sp.dma_start(cw[:], conv_w).then_inc(c_loaded, 16)
            sp.dma_start(cb[:], conv_b).then_inc(c_loaded, 16)
            sp.dma_start(ukR[:], w_uk).then_inc(c_loaded, 16)
            sp.dma_start(uvS[:], w_uv.rearrange("p h d -> p (h d)")).then_inc(c_loaded, 16)
            sp.dma_start(wpS[:], w_pool).then_inc(c_loaded, 16)
            done = Count()

            def load_to(end):
                while done.n < min(end, NU):
                    u = done.n
                    src, kts, cols = units[u]
                    if u >= NRING:
                        sp.wait_ge(w_lo, u - NRING + 1)
                    sp.dma_start(wraw[:, u % NRING, 0:kts, 0:cols], src).then_inc(w_loaded[u % NRING], 16)
                    done.up()

            for g in range(NBLK):
                load_to(unit_at["in", g] + 14)
                sp.wait_ge(kv_made, g + 1)
                for i in range(6):
                    sp.dma_start(key_store[i][g:g + 1].rearrange("b p n -> p b n"), key_columns(i, g, g + 1)).then_inc(kv_saved, 16)
                load_to(unit_at["o", g] + NRING)
                if g:
                    sp.wait_ge(unit_done, unit_at["ffn", g - 1] + len_ffn)
                    for i in (2, 3, 4, 5, 0, 1) if g + 1 < NBLK else (2, 3, 4, 5):
                        if i == 0:
                            sp.wait_ge(y_stored, 16 * JT * g)
                        sp.dma_start(key_columns(i, 0, g + 1), key_store[i][0:g + 1].rearrange("b p n -> p b n"))\
                            .then_inc(kv_loaded if i >= 2 else ki_loaded, 16)
            load_to(NU)

        @block.gpsimd
        def _(pool):
            step = Count()

            def link(ins):
                ins.then_inc(pool_step, 1)
                pool.wait_ge(pool_step, step.up())

            lows = Count()

            def weight_lows(end):
                while lows.n < min(end, NU):
                    u = lows.n
                    lows.up()
                    _, kts, cols = units[u]
                    s = u % NRING
                    pool.wait_ge(w_hi, u + 1)
                    if u >= NRING:
                        pool.wait_ge(unit_done, u - NRING + 1)
                    nc.gpsimd.tensor_tensor(wL[:, s, 0:kts, 0:cols], wraw[:, s, 0:kts, 0:cols],
                                            f(wH[:, s, 0:kts, 0:cols]), ALU.subtract).then_inc(w_lo, 1)

            link(nc.gpsimd.memset(ident[:], 0.0))
            link(nc.gpsimd.affine_select(out=ident[:], in_=ident[:], compare_op=ALU.not_equal, fill=1.0, base=0,
                                         pattern=[[-1, P]], channel_multiplier=1))
            nc.gpsimd.memset(ones[:], 1.0)
            nc.gpsimd.memset(uhalo[:], 0.0)
            nc.gpsimd.memset(ahalo[:], 0.0)
            for gi, win in enumerate(WINDOWS):
                for t in range(HALO):
                    nc.gpsimd.memset(invc[:, gi, t:t + 1], 1.0 / min(t + 1, win))
            nc.gpsimd.iota(distI[:], pattern=[[-1, SEQ]], base=DIST_BASE, channel_multiplier=1).then_inc(c_made, 1)
            def rows(b, j):
                return slice(b * TB + j * P, b * TB + (j + 1) * P)

            def outputs(b):
                pool.wait_ge(unit_done, unit_at["ffn", b] + len_ffn)
                pool.wait_ge(x1_ready, sums_after_ffn(b))
                pool.dma_start(gfin[:], g_final.rearrange("(a n) -> a n", a=1).to_broadcast([P, DM])).then_inc(gfin_loaded, 16)
                for j in range(JT):
                    pool.wait_ge(y_ready, JT * b + j + 1)
                    pool.dma_start(y[rows(b, j)], yb[:, j]).then_inc(y_stored, 16)

            index_slots = 0
            for j in range(JT):
                pool.dma_start(xa[:, j], x[rows(0, j)]).then_inc(x_loaded[j], 16)
            for g in range(NBLK):
                weight_lows(unit_at["in", g] + 14 + NRING)
                index_slots += sum(H * len(chunks(JT * g + j)) for j in range(JT))
                if g:
                    pool.wait_ge(lg_free, index_slots)
                    pool.wait_ge(x1_saved, 16 * JT * g)
                    for j in range(JT):
                        pool.dma_start(xb[:, j], x1_store[rows(g - 1, j)]).then_inc(x1_loaded[j], 16)
                    weight_lows(unit_at["ffn", g - 1] + len_ffn - KT + NRING)
                pool.wait_ge(q_hi, g + 1)
                nc.gpsimd.tensor_tensor(actL[:, 0:4, :], qF[:], f(actH[:, 0:4, :]), ALU.subtract)
                nc.gpsimd.tensor_tensor(actL[:, 4:8, :], poolF[:], f(actH[:, 4:8, :]), ALU.subtract).then_inc(q_lo, 1)
                if g:
                    weight_lows(unit_at["ffn", g - 1] + len_ffn + NRING)
                    outputs(g - 1)
                pool.wait_ge(o_lo, 2 * JT * (g + 1))
                if g + 1 < NBLK:
                    for j in range(JT):
                        pool.dma_start(xa[:, j], x[rows(g + 1, j)]).then_inc(x_loaded[j], 16)
                for j in range(JT):
                    pool.dma_start(xb[:, j], x[rows(g, j)]).then_inc(xr_loaded[j], 16)
                weight_lows(unit_at["o", g] + KT + NRING)
                if g + 1 < NBLK:
                    pool.wait_ge(x1_ready, sums_after_o(g))
                    for j in range(JT):
                        pool.dma_start(x1_store[rows(g, j)], xb[:, j]).then_inc(x1_saved, 16)
            weight_lows(NU)
            outputs(NBLK - 1)
            pool.wait_ge(y_stored, 16 * JT * NBLK)
            pool.wait_ge(kv_saved, 16 * 6 * NBLK)

        @block.tensor
        def _(pe):
            pj_kinds = []
            pj_release = {"act": pj_act, "dve": pj_dve, "stage": st_ready}
            tr_kinds = []
            tr_release = {"parts": tr_free, "residual": x1_ready, "sums": sums_copied}
            lgc, uc, lq, stc, turns = Count(), Count(), Count(), Count(), Count()

            def three(out, aH, aL, bH, bL, start, stop):
                nc.tensor.matmul(out, aL, bH, start=start, stop=False)
                nc.tensor.matmul(out, aH, bL, start=False, stop=False)
                return nc.tensor.matmul(out, aH, bH, start=False, stop=stop)

            def pj_slot(kind):
                k = len(pj_kinds)
                if k >= 4:
                    old = pj_kinds[k - 4]
                    n = pj_kinds[:k - 3].count(old)
                    pe.wait_ge(pj_release[old], n)
                pj_kinds.append(kind)
                return ps[:, k % 4]

            def pj_drained():
                for kind in pj_kinds[-4:]:
                    pe.wait_ge(pj_release[kind], pj_kinds.count(kind))

            def tr_slot(kind):
                k = len(tr_kinds)
                if k >= 2:
                    old = tr_kinds[k - 2]
                    pe.wait_ge(tr_release[old], tr_kinds[:k - 1].count(old))
                tr_kinds.append(kind)
                return ps[:, 4 + k % 2]

            def parts_made():
                pe.wait_ge(tr_free, tr_kinds.count("parts"))

            def next_unit():
                u = uc.n
                pe.wait_ge(w_lo, u + 1)
                uc.up()
                return u % NRING

            def down_pair(kts, gated):
                both = [(next_unit(), pj_slot("stage")) for _ in range(2)]
                for ks in (range(kts - 1), (kts - 1,)):
                    for s, out in both:
                        for k in ks:
                            pe.wait_ge(g_lo, gated + k + 1)
                            ins = three(out, wH[:, s, k, :], wL[:, s, k, :], gH[:, k, :], gL[:, k, :], k == 0, k == kts - 1)
                        if k == kts - 1:
                            ins.then_inc(unit_done, 1)

            def feature_unit(kind, rhsH, rhsL, kts):
                c = units[uc.n][2]
                s = next_unit()
                out = pj_slot(kind)[0:c]
                for k in range(kts):
                    ins = three(out, wH[:, s, k, 0:c], wL[:, s, k, 0:c], rhsH[:, k, :], rhsL[:, k, :], k == 0, k == kts - 1)
                ins.then_inc(unit_done, 1)

            def four_transposes(blocks):
                out = tr_slot("parts")
                for i, b in enumerate(blocks):
                    ins = nc.tensor.transpose(out[:, i * P:(i + 1) * P], b, ident[:])
                ins.then_inc(tr_full, 1)
                return ins

            norms = Count()

            def norm_transposes(src):
                pe.wait_ge(xn_ready, norms.up(JT))
                for k in range(KT):
                    four_transposes([src[:, j, k * P:(k + 1) * P] for j in range(JT)])
                parts_made()

            def ffn(b):
                norm_transposes(xn2)
                for t0, t1 in FF_PARTS:
                    for i in range(t0, t1):
                        feature_unit("act", actH, actL, KT)
                        feature_unit("act", actH, actL, KT)
                    down_pair(t1 - t0, NF * b + t0)
                    back_transposes(0)
                    for m in range(2, KT):
                        feature_unit("stage", gH, gL, t1 - t0)
                        back_transposes(m - 1)
                    back_transposes(KT - 1)

            def back_transposes(m):
                pe.wait_ge(st_ready, stc.up())
                out = tr_slot("residual")
                for j in range(JT):
                    ins = nc.tensor.transpose(out[:, j * P:(j + 1) * P], stage[:, m % 2, j * P:(j + 1) * P], ident[:])
                ins.then_inc(tr_full, 1)

            pe.wait_ge(c_made, 1)
            pe.wait_ge(c_lo, 1)
            for g in range(NBLK):
                norm_transposes(xn)
                for m in range(3):
                    feature_unit("act", actH, actL, KT)
                    if m == 1:
                        copied = pj_kinds.count("act")
                pe.wait_ge(pj_act, copied)
                four_transposes([cS[:, j * P:(j + 1) * P] for j in range(JT)])
                out = tr_slot("parts")
                for j in range(JT):
                    ins = nc.tensor.transpose(out[:, j * KW:(j + 1) * KW], kwS[:, j * P:(j + 1) * P], ident[0:KW, 0:KW])
                ins.then_inc(tr_full, 1)
                for m in range(2):
                    feature_unit("act", actH, actL, KT)
                pe.wait_ge(tok_ready, g + 1)
                four_transposes([cF[:, j, :] for j in range(JT)])
                feature_unit("act", actH, actL, KT)
                for m in range(4):
                    feature_unit("dve", actH, actL, KT)
                for m in range(4):
                    feature_unit("act", actH, actL, KT)
                for m in range(4):
                    pe.wait_ge(pool_ready, 4 * g + m + 1)
                    out = pj_slot("act")
                    three(out, wpH[:, m, :], wpL[:, m, :], pH[:, m, :], pL[:, m, :], True, True).then_inc(pooled_full, 1)
                pj_drained()
                parts_made()
                if g > 1:
                    pe.wait_ge(ki_loaded, 16 * 2 * (g - 1))
                for j in range(JT):
                    t = JT * g + j
                    for h in range(H):
                        for a, n in chunks(t):
                            k = lgc.n
                            if k >= NLG:
                                pe.wait_ge(lg_free, k - NLG + 1)
                            lgc.up()
                            out = lg(k, n)
                            for b in range(0, n, 512):
                                e = min(n, b + 512)
                                q = qiS[:, h, j * P:(j + 1) * P]
                                nc.tensor.matmul(out[:, b:e], q, kiL[:, a + b:a + e], start=True, stop=False)
                                ins = nc.tensor.matmul(out[:, b:e], q, kiH[:, a + b:a + e], start=False, stop=True)
                            ins.then_inc(lg_full, 1)

                pe.wait_ge(lg_free, lgc.n)
                if g:
                    ffn(g - 1)
                    pj_drained()
                made = {}

                def query(j):
                    for r in range(2):
                        out = tr_slot("parts")
                        for i in range(4):
                            ins = three(out[:, i * P:(i + 1) * P], ukH[:, 4 * r + i, :], ukL[:, 4 * r + i, :],
                                        actH[:, 2 * r + i // 2, j * P:(j + 1) * P],
                                        actL[:, 2 * r + i // 2, j * P:(j + 1) * P], True, True)
                        ins.then_inc(tr_full, 1)
                    made[("query", j)] = tr_kinds.count("parts")

                def logits(n, q):
                    j, h = divmod(n, H)
                    if h == 0 and q == 0:
                        pe.wait_ge(tr_free, made[("query", j)])
                    k = lq.n
                    if k >= 2:
                        pe.wait_ge(ttr_done, k - 1)
                    a, m = quad(g, n, q)
                    keys_ = slice(a * P, (a + m) * P)
                    three(ps[:, k % 2, 0:m * P], qlH[j % 2][:, h, :], qlL[j % 2][:, h, :], cTH[:, keys_], cTL[:, keys_],
                          True, True).then_inc(lq_full, 1)
                    lq.up()

                def turn(n, q):
                    pe.wait_ge(exp_done, turns.up())
                    a, m = quad(g, n, q)
                    out = tr_slot("parts")
                    pr = prob_row(g, n)
                    for i in range(m):
                        ins = nc.tensor.transpose(out[:, i * P:(i + 1) * P], pr[:, (a + i) * P:(a + i + 1) * P], ident[:])
                    ins.then_inc(tr_full, 1)
                    made[(n, q)] = (tr_kinds.count("parts"), turns.n - 1)

                def value(n, q):
                    j, h = divmod(n, H)
                    G = 8 * g + n // 4
                    if n % 4 == 0 and q == 0 and G >= 2:
                        pe.wait_ge(o_free, G - 1)
                    count, k = made[(n, q)]
                    pe.wait_ge(tr_free, count)
                    a, m = quad(g, n, q)
                    b = k % 2
                    out = o_banks(G)[:, h % 4]
                    for i in range(m):
                        both = pt[:, b, :, i * P:(i + 1) * P]
                        nc.tensor.matmul(out, cL[:, a + i, :], both, start=(a + i == 0), stop=False)
                        ins = nc.tensor.matmul(out, cH[:, a + i, :], both, start=False, stop=(a + i == JT * g + j))
                    ins.then_inc(pv_done, 1)

                def sums(G):
                    pe.wait_ge(dg_ready, 8 * g + G + 1)
                    nc.tensor.matmul(tr_slot("sums"), ones[:], dgR[:].rearrange("p a b -> p (a b)"),
                                     start=True, stop=True).then_inc(tr_full, 1)

                def out_heads(G):
                    pe.wait_ge(o_lo, 8 * g + G + 1)
                    out = tr_slot("parts")
                    for pp in range(2):
                        c = (2 * (G % 2) + pp) * P
                        ins = three(out[:, pp * 256:pp * 256 + 256], uvH[:, c:c + P], uvL[:, c:c + P],
                                    oH[:, 2 * pp:2 * pp + 2, :].rearrange("p a b -> p (a b)"),
                                    oL[:, 2 * pp:2 * pp + 2, :].rearrange("p a b -> p (a b)"), True, True)
                    ins.then_inc(tr_full, 1)

                pe.wait_ge(q_lo, g + 1)
                if g:
                    pe.wait_ge(kv_loaded, 16 * 4 * g)
                do = {"query": query, "logits": logits, "turn": turn, "value": value, "sums": sums, "out": out_heads}
                for kind, *at in value_steps(g):
                    if kind in do:
                        do[kind](*at)
                parts_made()
                pe.wait_ge(ttr_done, lq.n)

                for m in range(KT):
                    feature_unit("stage", actH, actL, KT)
                    if m:
                        back_transposes(m - 1)
                back_transposes(KT - 1)
            ffn(NBLK - 1)

        @block.scalar
        def _(act):
            hi, pj, tr, lgc, var, ptc, biases = Count(), Count(), Count(), Count(), Count(), Count(), Count()

            def weight_highs(upto):
                while hi.n < min(upto, NU):
                    u = hi.n
                    _, kts, cols = units[u]
                    s = u % NRING
                    act.wait_ge(w_loaded[s], 16 * (u // NRING + 1))
                    if u >= NRING:
                        act.wait_ge(unit_done, u - NRING + 1)
                    nc.scalar.activation(wH[:, s, 0:kts, 0:cols], wraw[:, s, 0:kts, 0:cols], ACT.Copy).then_inc(w_hi, 1)
                    hi.up()

            def pj_wait(u):
                act.wait_ge(unit_done, u + 1)
                weight_highs(u + 1 + NRING)
                k = pj.n
                pj.up()
                return ps[:, k % 4]

            def square_sums(src, junk, loaded=None, count=0):
                for j in range(JT):
                    if loaded:
                        act.wait_ge(loaded[j], 16 * count)
                    nc.scalar.activation(junk[:, j], src[:, j], ACT.Square, accum_out=st[:, j:j + 1]).then_inc(sq_done, 1)

            def root():
                act.wait_ge(var_ready, var.up())
                nc.scalar.activation(st[:, 8:12], st[:, 4:8], ACT.Sqrt).then_inc(std_ready, 1)

            def tr_high(dst, scale=None):
                act.wait_ge(tr_full, tr.n + 1)
                src = ps[:, 4 + tr.n % 2, 0:dst.shape[1]]
                tr.up()
                if scale is None:
                    nc.scalar.activation(dst, src, ACT.Copy).then_inc(tr_hi, 1)
                else:
                    nc.scalar.activation(dst, src, ACT.Copy, scale=scale).then_inc(tr_hi, 1)

            act.wait_ge(c_loaded, 16 * NCONST)
            act.wait_ge(uk_scaled, H)
            nc.scalar.activation(ukH[:], ukS[:], ACT.Copy).then_inc(c_hi, 1)
            nc.scalar.activation(uvH[:], uvS[:], ACT.Copy).then_inc(c_hi, 1)
            nc.scalar.activation(wpH[:], wpS[:], ACT.Copy).then_inc(c_hi, 1)
            act.wait_ge(c_lo, 1)
            weight_highs(NRING)
            def stages(first_unit):
                for m in range(KT):
                    bank = pj_wait(first_unit + m)
                    if m >= 2:
                        act.wait_ge(tr_full, tr.n + m - 1)
                    nc.scalar.activation(stage[:, m % 2, :], bank, ACT.Copy).then_inc(st_ready, 1)
                tr.up(KT)

            def query_highs():
                nc.scalar.activation(actH[:, 0:4, :], qF[:], ACT.Copy)
                nc.scalar.activation(actH[:, 4:8, :], poolF[:], ACT.Copy).then_inc(q_hi, 1)

            def ffn(b):
                if b + 1 < NBLK:
                    act.wait_ge(kv_saved, 16 * 6 * (b + 2))
                    square_sums(xb, xn2, x1_loaded, b + 1)
                else:
                    act.wait_ge(x1_ready, sums_after_o(b))
                    square_sums(xb, xn2)
                root()
                for k in range(KT):
                    tr_high(actH[:, k, :], gf[:, k:k + 1])
                act.wait_ge(pj_act, 14 * min(b + 2, NBLK) + 2 * NF * b)
                u = unit_at["ffn", b]

                def conv_input(i, s, u):
                    c = i + s * NF
                    bank = pj_wait(u)
                    n = NF * b + i
                    if n:
                        act.wait_ge(taps_done, 2 * (n - 1) + s + 1)
                    if n >= 2:
                        act.wait_ge(g_lo, n - 1)
                    nc.scalar.activation(asb[:, s, 0:2], ahalo[:, b % 2, c, :], ACT.Copy)
                    nc.scalar.activation(asb[:, s, 2:], bank, ACT.Copy)
                    nc.scalar.activation(acc[:, n % 2, s, :], bank, ACT.Identity, bias=cb[:, c:c + 1],
                                         scale=cw[:, 2, c:c + 1]).then_inc(conv_in, 1)
                    nc.scalar.activation(ahalo[:, (b + 1) % 2, c, :], bank[:, TB - 2:TB], ACT.Copy).then_inc(pj_act, 1)

                def gate_tanh(i):
                    n = NF * b + i
                    act.wait_ge(taps_done, 2 * n + 1)
                    if n:
                        act.wait_ge(gu_ready, n)
                    nc.scalar.activation(th[:], acc[:, n % 2, 0, :], ACT.Tanh, scale=0.5).then_inc(tanh_done, 1)

                def gated_high(i, t0):
                    n = NF * b + i
                    act.wait_ge(gu_ready, n + 1)
                    nc.scalar.activation(gH[:, i - t0, :], acc[:, n % 2, 1, :], ACT.Copy).then_inc(g_hi, 1)

                for t0, t1 in FF_PARTS:
                    for i in range(t0, t1):
                        conv_input(i, 0, u)
                        if i > t0:
                            gate_tanh(i - 1)
                        conv_input(i, 1, u + 1)
                        if i > t0:
                            gated_high(i - 1, t0)
                        u += 2
                    gate_tanh(t1 - 1)
                    gated_high(t1 - 1, t0)
                    if t1 == NF and b + 1 < NBLK:
                        query_highs()
                    stages(u)
                    u += KT
                act.wait_ge(x1_ready, sums_after_ffn(b))
                square_sums(xb, yb)
                root()

            square_sums(xa, xn, x_loaded, 1)
            root()
            for g in range(NBLK):
                u0 = unit_at["in", g]
                for k in range(KT):
                    tr_high(actH[:, k, :], gm[:, k:k + 1])
                def pool_channels(m):
                    bank = pj_wait(u0 + 2 + m)
                    nc.scalar.activation(uT[:, m, HALO:], bank, ACT.Copy).then_inc(pj_act, 1)

                bank = pj_wait(u0)
                nc.scalar.activation(cS[:], bank, ACT.Copy).then_inc(pj_act, 1)
                bank = pj_wait(u0 + 1)
                for r in range(2):
                    nc.scalar.activation(kiH[r * DH:(r + 1) * DH, g * TB:(g + 1) * TB], bank[0:DH], ACT.Copy)
                nc.scalar.activation(kwS[:], bank[0:KW], ACT.Copy).then_inc(pj_act, 1)
                pool_channels(0)
                act.wait_ge(tr_full, tr.n + 1)
                bank = ps[:, 4 + tr.n % 2]
                tr.up(2)
                for j in range(JT):
                    nc.scalar.activation(cF[:, j, :], bank[:, j * CL:(j + 1) * CL], ACT.Square,
                                         accum_out=st[:, j:j + 1]).then_inc(csq_done, 1)
                root()
                pool_channels(1)
                pool_channels(2)
                act.wait_ge(tok_ready, g + 1)
                tr_high(cTH[:, g * TB:(g + 1) * TB])
                nc.scalar.activation(cH[:, JT * g:JT * g + JT, :], cF[:], ACT.Copy).then_inc(cF_hi, 1)
                pool_channels(3)
                if g:
                    act.wait_ge(x1_saved, 16 * JT * g)
                for m in range(4):
                    bank = pj_wait(u0 + 6 + m)
                    nc.scalar.activation(qiS[0:64, 2 * m, :], bank[0:64], ACT.Copy).then_inc(pj_hi, 1)
                    nc.scalar.activation(qiS[0:64, 2 * m + 1, :], bank[64:128], ACT.Copy).then_inc(pj_hi, 1)
                for m in range(4):
                    bank = pj_wait(u0 + 10 + m)
                    nc.scalar.activation(qF[:, m, :], bank, ACT.Copy).then_inc(pj_act, 1)
                for m in range(4):
                    act.wait_ge(pooled_full, 4 * g + m + 1)
                    bank = ps[:, pj.n % 4]
                    pj.up()
                    nc.scalar.activation(poolF[:, m, :], bank, ACT.Copy, scale=psc[:, m:m + 1]).then_inc(pj_act, 1)
                for j in range(JT):
                    t = JT * g + j
                    for h in range(H):
                        for a, n in chunks(t):
                            act.wait_ge(lg_full, lgc.n + 1)
                            s = lg(lgc.n, n)
                            lgc.up()
                            nc.scalar.activation(s, s, ACT.Relu, scale=wabs[:, j, h:h + 1]).then_inc(relu_done, 1)

                if g:
                    ffn(g - 1)
                else:
                    query_highs()
                Q = g + 1

                def exponentials(n, q):
                    if q == 0:
                        act.wait_ge(nb_ready, biases.up())
                    a, m = quad(g, n, q)
                    pr = prob_row(g, n)[:, a * P:(a + m) * P]
                    h = n % H
                    nc.scalar.activation(pr, pr, ACT.Exp, bias=nb[:, n % 4:n % 4 + 1], scale=2.0 ** -(h + 1),
                                         accum_out=lsum[:, (n // 4) % 2, n % 4, q:q + 1]).then_inc(exp_done, 1)

                def query(j):
                    for r in range(2):
                        tr_high(qlH[j % 2][:, 4 * r:4 * r + 4, :].rearrange("p a b -> p (a b)"))

                def turn(n, q):
                    if ptc.n >= 2:
                        act.wait_ge(pv_done, ptc.n - 1)
                    _, m = quad(g, n, q)
                    tr_high(pt[:, ptc.n % 2, 0, 0:m * P])
                    ptc.up()
                    if q + 1 < Q:
                        exponentials(n, q + 1)
                    elif n + 1 < JT * H:
                        exponentials(n + 1, 0)

                def sums(G):
                    act.wait_ge(tr_full, tr.n + 1)
                    src = ps[:, 4 + tr.n % 2]
                    tr.up()
                    nc.scalar.activation(dgR[:].rearrange("p a b -> p (a b)"), src, ACT.Copy).then_inc(sums_copied, 1)

                def norm(G):
                    act.wait_ge(o_free, 8 * g + G + 1)
                    nc.scalar.activation(oH[:], dgR[:], ACT.Copy).then_inc(o_hi, 1)

                def out_heads(G):
                    act.wait_ge(tr_full, tr.n + 1)
                    j, hg = divmod(G, 2)
                    for r in range(2):
                        rows = slice(64 * r, 64 * r + 64)
                        src = ps[rows, 4 + tr.n % 2].rearrange("p (a b) -> p a b", a=2)[:, :, r * P:(r + 1) * P]
                        ins = nc.scalar.activation(actH[rows, 2 * hg:2 * hg + 2, j * P:(j + 1) * P], src, ACT.Copy)
                    ins.then_inc(tr_hi, 1)
                    tr.up()

                do = {"query": query, "turn": turn, "sums": sums, "norm": norm, "out": out_heads}
                first = True
                for kind, *at in value_steps(g):
                    if kind == "turn" and first:
                        exponentials(0, 0)
                        first = False
                    if kind in do:
                        do[kind](*at)

                if g + 1 < NBLK:
                    square_sums(xa, xn, x_loaded, g + 2)
                    root()
                stages(unit_at["o", g])
            ffn(NBLK - 1)

        @block.vector
        def _(dve):
            step, pj, tr, tr_parts, trh, lgc, relu, pjh, sqc, stdc, ptq, lq = [Count() for _ in range(12)]

            def link(ins):
                ins.then_inc(dve_step, 1)
                dve.wait_ge(dve_step, step.up())

            def rstd(width):
                nc.vector.tensor_scalar(st[:, 4:8], st[:, 0:4], 1.0 / width, EPS, ALU.mult, ALU.add).then_inc(var_ready, 1)
                dve.wait_ge(std_ready, stdc.up())
                link(nc.vector.reciprocal(st[:, 12:16], st[:, 8:12]))
                link(nc.vector.tensor_tensor(st[:, 16:20], st[:, 12:16], st[:, 12:16], ALU.mult))
                link(nc.vector.tensor_tensor(st[:, 16:20], st[:, 16:20], st[:, 4:8], ALU.mult))
                link(nc.vector.tensor_scalar(st[:, 16:20], st[:, 16:20], -0.5, 1.5, ALU.mult, ALU.add))
                link(nc.vector.tensor_tensor(st[:, 12:16], st[:, 12:16], st[:, 16:20], ALU.mult))

            def tr_low(dst, dstH, scale=None):
                dve.wait_ge(tr_hi, trh.up())
                n = dst.shape[1]
                src = ps[:, 4 + tr.n % 2, 0:n]
                tr.up()
                tr_parts.up()
                if scale is None:
                    nc.vector.tensor_tensor(dst, src, f(dstH), ALU.subtract).then_inc(tr_free, 1)
                else:
                    nc.vector.scalar_tensor_tensor(dst, src, scale, f(dstH), ALU.mult, ALU.subtract).then_inc(tr_free, 1)

            def normed(dst, src):
                dve.wait_ge(sq_done, JT * sqc.up())
                rstd(DM)
                for j in range(JT):
                    nc.vector.tensor_scalar(dst[:, j], src[:, j], st[:, 12 + j:13 + j], None, ALU.mult).then_inc(xn_ready, 1)

            def normed_lows(scales):
                for k in range(KT):
                    tr_low(actL[:, k, :], actH[:, k, :], scales[:, k:k + 1])

            dve.wait_ge(c_made, 1)
            link(nc.vector.tensor_copy(distF[:], distI[:]))
            link(nc.vector.tensor_scalar(distN[:], distF[:], -1.0, None, ALU.mult))
            link(nc.vector.tensor_tensor(dist[:], distF[:], distN[:], ALU.max))
            dve.wait_ge(c_loaded, 16 * NCONST)
            link(nc.vector.memset(ukS[:], 0.0))
            for h in range(H):
                rows = slice(64 * (h % 2), 64 * (h % 2) + 64)
                nc.vector.tensor_scalar(ukS[rows, h, :], ukR[rows, h // 2, :], DH ** -0.5 * 2.0 ** (h + 1), None,
                                        ALU.mult).then_inc(uk_scaled, 1)
            dve.wait_ge(uk_scaled, H)
            dve.wait_ge(c_hi, 3)
            link(nc.vector.tensor_tensor(ukL[:], ukS[:], f(ukH[:]), ALU.subtract))
            link(nc.vector.tensor_tensor(uvL[:], uvS[:], f(uvH[:]), ALU.subtract))
            nc.vector.tensor_tensor(wpL[:], wpS[:], f(wpH[:]), ALU.subtract).then_inc(c_lo, 1)
            dve.wait_ge(c_lo, 1)
            def count(g, j, thr, op=ALU.is_ge):
                n = keys(JT * g + j)
                nc.vector.tensor_scalar(counted[:, j, 0:n], score[:, j, 0:n], thr, None, op, ALU.add,
                                        accum_out=cnt[:, j:j + 1]).then_inc(dve_step, 1)
                step.up()

            def search(g):
                tiles = [j for j in range(JT) if JT * g + j >= 2]
                a, b = tiles[0], JT
                for j in tiles:
                    count(g, j, 0.0)
                    yield
                dve.wait_ge(dve_step, step.n)
                link(nc.vector.tensor_scalar(drop[:, a:b].bitcast(I32), cnt[:, a:b], float(TOPK), -1.0, ALU.is_lt, ALU.mult))
                nc.vector.tensor_scalar(cand[:, a:b], drop[:, a:b], 1 << 30, None, ALU.bitwise_xor).then_inc(dve_step, 1)
                made = step.up()
                yield
                for bit in range(30, -1, -1):
                    dve.wait_ge(dve_step, made)
                    for j in tiles:
                        count(g, j, cand[:, j:j + 1].bitcast(F32))
                        counts = step.n
                        yield
                    dve.wait_ge(dve_step, counts)
                    nc.vector.tensor_scalar(drop[:, a:b].bitcast(I32), cnt[:, a:b], float(TOPK), float(1 << bit),
                                            ALU.is_lt, ALU.mult).then_inc(dve_step, 1)
                    dropped = step.up()
                    yield
                    dve.wait_ge(dve_step, dropped)
                    if bit:
                        ins = nc.vector.scalar_tensor_tensor(cand[:, a:b], cand[:, a:b], 1 << (bit - 1), drop[:, a:b],
                                                             ALU.bitwise_xor, ALU.bitwise_xor)
                    else:
                        ins = nc.vector.tensor_tensor(cand[:, a:b], cand[:, a:b], drop[:, a:b], ALU.bitwise_xor)
                    ins.then_inc(dve_step, 1)
                    made = step.up()
                    yield
                dve.wait_ge(dve_step, made)

            def mask(g):
                def then(ins):
                    ins.then_inc(dve_step, 1)
                    return step.up()

                for j in range(JT):
                    t = JT * g + j
                    n = keys(t)
                    o = DIST_BASE - P * t
                    if t < 2:
                        link(nc.vector.tensor_copy(score[:, j, 0:n], dist[:, o:o + n]))
                        nc.vector.memset(score[0:64, j, n - 64:n], BIG).then_inc(d_ready, 1)
                        continue
                    v = cand[:, j:j + 1].bitcast(F32)
                    sc, eq, tie, rk = score[:, j, 0:n], eqm[:, 0:n], tiem[:, 0:n], rank[:, 0:n]
                    if j:
                        dve.wait_ge(d_ready, JT * g + j)
                    then(nc.vector.tensor_scalar(tie, sc, v, None, ALU.is_gt, ALU.add, accum_out=need[:, 0:1]))
                    yield
                    made = then(nc.vector.tensor_scalar(eq, sc, v, None, ALU.is_equal))
                    yield
                    dve.wait_ge(dve_step, made)
                    then(nc.vector.tensor_scalar(need[:, 1:2], need[:, 0:1], -1.0, float(TOPK), ALU.mult, ALU.add))
                    made = then(nc.vector.tensor_tensor_scan(rk, eq, eq, 0.0, ALU.add, ALU.max))
                    yield
                    dve.wait_ge(dve_step, made)
                    made = then(nc.vector.scalar_tensor_tensor(tie, rk, need[:, 1:2], eq, ALU.is_le, ALU.mult))
                    yield
                    dve.wait_ge(dve_step, made)
                    made = then(nc.vector.scalar_tensor_tensor(eq, sc, v, tie, ALU.is_le, ALU.subtract))
                    yield
                    dve.wait_ge(dve_step, made)
                    nc.vector.scalar_tensor_tensor(sc, eq, BIG, dist[:, o:o + n], ALU.mult, ALU.max).then_inc(d_ready, 1)
                    yield

            def threshold_and_mask(g):
                yield from search(g)
                yield from mask(g)

            def go_on(work, n):
                for _ in range(n):
                    next(work, None)

            def residual(work, n):
                for m in range(KT):
                    dve.wait_ge(tr_full, tr.n + 1)
                    src = ps[:, 4 + tr.n % 2].rearrange("p (j c) -> p j c", j=JT)
                    tr.up()
                    dst = xb[:, :, m * P:(m + 1) * P]
                    nc.vector.tensor_tensor(dst, src, dst, ALU.add).then_inc(x1_ready, 1)
                    go_on(work, n + (m % 2))

            def ffn(b, work):
                go_on(work, 6)
                normed(xn2, xb)
                normed_lows(gf)

                def taps(i, s, hurry):
                    n = NF * b + i
                    c = i + s * NF
                    dve.wait_ge(conv_in, 2 * n + s + 1)
                    d = acc[:, n % 2, s, :]
                    nc.vector.scalar_tensor_tensor(d, asb[:, s, 1:TB + 1], cw[:, 1, c:c + 1], d, ALU.mult,
                                                   ALU.add).then_inc(dve_step, 1)
                    tap = step.up()
                    go_on(work, 0 if hurry else 1)
                    dve.wait_ge(dve_step, tap)
                    nc.vector.scalar_tensor_tensor(d, asb[:, s, 0:TB], cw[:, 0, c:c + 1], d, ALU.mult,
                                                   ALU.add).then_inc(taps_done, 1)

                def gate(i, hurry):
                    n = NF * b + i
                    dve.wait_ge(tanh_done, n + 1)
                    dve.wait_ge(taps_done, 2 * n + 2)
                    nc.vector.scalar_tensor_tensor(th[:], th[:], 1.0, acc[:, n % 2, 0, :], ALU.add,
                                                   ALU.mult).then_inc(dve_step, 1)
                    opened = step.up()
                    go_on(work, 0 if hurry else 1)
                    dve.wait_ge(dve_step, opened)
                    nc.vector.scalar_tensor_tensor(acc[:, n % 2, 1, :], th[:], 0.5, acc[:, n % 2, 1, :], ALU.mult,
                                                   ALU.mult).then_inc(gu_ready, 1)

                def gate_low(i, t0):
                    n = NF * b + i
                    dve.wait_ge(g_hi, n + 1)
                    nc.vector.tensor_tensor(gL[:, i - t0, :], acc[:, n % 2, 1, :], f(gH[:, i - t0, :]),
                                            ALU.subtract).then_inc(g_lo, 1)

                for t0, t1 in FF_PARTS:
                    for i in range(t0, t1):
                        last = i == t1 - 1
                        taps(i, 0, last)
                        if i > t0:
                            gate(i - 1, False)
                        go_on(work, 1)
                        taps(i, 1, last)
                        if i > t0:
                            gate_low(i - 1, t0)
                        go_on(work, 0 if last else 2)
                    gate(t1 - 1, True)
                    gate_low(t1 - 1, t0)
                    residual(work, 3)
                dve.wait_ge(sq_done, JT * sqc.up())
                rstd(DM)
                dve.wait_ge(gfin_loaded, 16 * (b + 1))
                for j in range(JT):
                    nc.vector.scalar_tensor_tensor(yb[:, j], xb[:, j], st[:, 12 + j:13 + j], gfin[:], ALU.mult,
                                                   ALU.mult).then_inc(y_ready, 1)

            normed(xn, xa)
            for g in range(NBLK):
                normed_lows(gm)
                tiles = slice(JT * g, JT * (g + 1))
                block_keys = slice(g * TB, (g + 1) * TB)
                dve.wait_ge(pj_act, 14 * g + 2 * NF * max(g - 1, 0) + 2)
                for r in range(2):
                    rows = slice(r * DH, (r + 1) * DH)
                    nc.vector.tensor_tensor(kiL[rows, block_keys], kwS[0:DH, :], f(kiH[rows, block_keys]), ALU.subtract)
                link(nc.vector.tensor_copy(uT[:, :, 0:HALO], uhalo[:]))
                dve.wait_ge(csq_done, 4 * (g + 1))
                rstd(CL)
                bank = ps[:, 4 + tr.n % 2]
                for j in range(JT):
                    ins = nc.vector.scalar_tensor_tensor(cF[:, j, :], bank[:, j * CL:(j + 1) * CL], st[:, 12 + j:13 + j],
                                                         gkv[:], ALU.mult, ALU.mult)
                ins.then_inc(tr_free, 1)
                tr.up()
                dve.wait_ge(tr_full, tr.n + 1)
                bank = ps[:, 4 + tr.n % 2, 0:JT * KW].rearrange("p (j n) -> p j n", n=KW)[:, :, DH:KW]
                link(nc.vector.tensor_scalar(wS[:], bank, H ** -0.5 * DH ** -0.5, None, ALU.mult))
                nc.vector.tensor_scalar(wsgn[:], wS[:], 0.0, 2.0, ALU.is_ge, ALU.mult).then_inc(tr_free, 1)
                tr.up()
                dve.wait_ge(tr_free, tr_parts.up(2))
                link(nc.vector.tensor_scalar(wsgn[:], wsgn[:], -1.0, None, ALU.add))
                nc.vector.tensor_tensor(wabs[:], wS[:], wsgn[:], ALU.mult).then_inc(tok_ready, 1)

                def pooling(m, win):
                    dve.wait_ge(pj_act, 14 * g + 2 * NF * max(g - 1, 0) + 2 + m + 1)
                    src, free, lo = uT[:, m, :], [s0[:], s1[:]], 0
                    for sh in [d for d in (1, 2, 4, 8) if d < win]:
                        lo += sh
                        link(nc.vector.tensor_tensor(free[0][:, lo:], src[:, lo:], src[:, lo - sh:HALO + TB - sh], ALU.add))
                        src, free = free[0], free[::-1]
                    other = free[0]
                    link(nc.vector.scalar_tensor_tensor(other[:, HALO:], src[:, HALO:], 1.0 / win, uT[:, m, HALO:],
                                                        ALU.mult, ALU.subtract))
                    if g == 0:
                        e = HALO + HALO
                        link(nc.vector.tensor_tensor(other[:, HALO:e], src[:, HALO:e], invc[:, m, :], ALU.mult))
                        link(nc.vector.tensor_tensor(other[:, HALO:e], other[:, HALO:e], uT[:, m, HALO:e], ALU.subtract))
                    link(nc.vector.tensor_copy(pH[:, m, :], other[:, HALO:]))
                    nc.vector.tensor_tensor(pL[:, m, :], other[:, HALO:], f(pH[:, m, :]), ALU.subtract).then_inc(pool_ready, 1)
                    dve.wait_ge(pool_ready, 4 * g + m + 1)

                pj.up(6)
                for m, win in enumerate(WINDOWS):
                    pooling(m, win)
                    if m == 0:
                        tr_low(cTL[:, block_keys], cTH[:, block_keys])
                        dve.wait_ge(cF_hi, g + 1)
                        nc.vector.tensor_tensor(cL[:, tiles, :], cF[:], f(cH[:, tiles, :]), ALU.subtract).then_inc(kv_made, 1)
                    dve.wait_ge(pj_hi, pjh.up(2))
                    bank = ps[:, pj.n % 4]
                    pj.up()
                    nc.vector.tensor_tensor(qiS[64:128, 2 * m, :], bank[0:64], f(qiS[0:64, 2 * m, :]), ALU.subtract)
                    nc.vector.tensor_tensor(qiS[64:128, 2 * m + 1, :], bank[64:128], f(qiS[0:64, 2 * m + 1, :]),
                                            ALU.subtract).then_inc(pj_dve, 1)
                link(nc.vector.tensor_copy(uhalo[:], uT[:, :, TB:TB + HALO]))
                pj.up(8)
                for j in range(JT):
                    t = JT * g + j
                    for h in range(H):
                        nch = len(chunks(t))
                        for a, n in chunks(t):
                            dve.wait_ge(relu_done, relu.up())
                            s = lg(lgc.n, n)
                            lgc.up()
                            dst = score[:, j, a:a + n]
                            if h == 0:
                                nc.vector.tensor_scalar(dst, s, wsgn[:, j, 0:1], None, ALU.mult).then_inc(lg_free, 1)
                            else:
                                dve.wait_ge(lg_free, lgc.n - nch)
                                nc.vector.scalar_tensor_tensor(dst, s, wsgn[:, j, h:h + 1], dst, ALU.mult,
                                                               ALU.add).then_inc(lg_free, 1)
                    if t >= 2:
                        dve.wait_ge(lg_free, lgc.n)
                        link(nc.vector.memset(score[0:64, j, keys(t) - 64:keys(t)], -FLT_MAX))
                work = threshold_and_mask(g)
                if g:
                    ffn(g - 1, work)
                    pj.up(len_ffn)
                    dve.wait_ge(y_ready, JT * g)
                for _ in work:
                    pass
                dve.wait_ge(d_ready, JT * (g + 1))

                Q = g + 1

                def query(j):
                    for r in range(2):
                        hs = slice(4 * r, 4 * r + 4)
                        tr_low(qlL[j % 2][:, hs, :].rearrange("p a b -> p (a b)"), qlH[j % 2][:, hs, :].rearrange("p a b -> p (a b)"))

                def logits(n, q):
                    j, h = divmod(n, H)
                    a, m = quad(g, n, q)
                    dve.wait_ge(lq_full, lq.n + 1)
                    s = n % 4
                    if q:
                        dve.wait_ge(ttr_done, lq.n)
                    nc.vector.tensor_tensor_reduce(prob_row(g, n)[:, a * P:(a + m) * P], ps[:, lq.n % 2, 0:m * P],
                                                   score[:, j, a * P:(a + m) * P], 1.0,
                                                   mx[:, s, q - 1:q] if q else -FLT_MAX, ALU.subtract, ALU.max,
                                                   mx[:, s, q:q + 1]).then_inc(ttr_done, 1)
                    lq.up()
                    if q == Q - 1:
                        dve.wait_ge(ttr_done, lq.n)
                        nc.vector.tensor_scalar(nb[:, s:s + 1], mx[:, s, q:q + 1], -(2.0 ** -(h + 1)), None,
                                                ALU.mult).then_inc(nb_ready, 1)

                def turn(n, q):
                    _, m = quad(g, n, q)
                    b = ptq.n % 2
                    tr_low(pt[:, b, 1, 0:m * P], pt[:, b, 0, 0:m * P])
                    ptq.up()

                def recip(G):
                    ls = lsum[:, G % 2, :, 0:Q]
                    if Q > 1:
                        link(nc.vector.tensor_reduce(rl[:], ls, mybir.AxisListType.X, ALU.add))
                        link(nc.vector.reciprocal(rl[:], rl[:]))
                    else:
                        link(nc.vector.reciprocal(rl[:], lsum[:, G % 2, :, 0]))
                    nc.vector.tensor_tensor(dgR[:], ident[:].unsqueeze(1).to_broadcast([P, 4, P]),
                                            rl[:].unsqueeze(2).to_broadcast([P, 4, P]), ALU.mult).then_inc(dg_ready, 1)

                def sums(G):
                    dve.wait_ge(sums_copied, 8 * g + G + 1)
                    tr.up()
                    dve.wait_ge(pv_done, valued[G])
                    o = o_banks(8 * g + G)
                    link(nc.vector.tensor_tensor(o[:, :, 1, :], o[:, :, 1, :], dgR[:], ALU.mult))
                    link(nc.vector.tensor_tensor(dgR[:], o[:, :, 0, :], dgR[:], ALU.mult))
                    nc.vector.tensor_tensor(dgR[:], o[:, :, 1, :], dgR[:], ALU.add).then_inc(o_free, 1)

                def norm(G):
                    dve.wait_ge(o_hi, 8 * g + G + 1)
                    nc.vector.tensor_tensor(oL[:], dgR[:], f(oH[:]), ALU.subtract).then_inc(o_lo, 1)

                def out_heads(G):
                    j, hg = divmod(G, 2)
                    dve.wait_ge(tr_hi, trh.up())
                    for r in range(2):
                        rows = slice(64 * r, 64 * r + 64)
                        src = ps[rows, 4 + tr.n % 2].rearrange("p (a b) -> p a b", a=2)[:, :, r * P:(r + 1) * P]
                        ins = nc.vector.tensor_tensor(actL[rows, 2 * hg:2 * hg + 2, j * P:(j + 1) * P], src,
                                                      f(actH[rows, 2 * hg:2 * hg + 2, j * P:(j + 1) * P]), ALU.subtract)
                    ins.then_inc(tr_free, 1)
                    tr.up()
                    tr_parts.up()

                valued = [ptq.n + 4 * Q * (G + 1) for G in range(2 * JT)]
                do = {"query": query, "logits": logits, "turn": turn, "recip": recip, "sums": sums, "norm": norm,
                      "out": out_heads}
                for kind, *at in value_steps(g):
                    if kind in do:
                        do[kind](*at)

                if g + 1 < NBLK:
                    normed(xn, xa)
                for j in range(JT):
                    dve.wait_ge(xr_loaded[j], 16 * (g + 1))
                residual(iter(()), 0)
                pj.up(KT)
            ffn(NBLK - 1, iter(()))


_NAMES = ["x", "g_mix", "w_in", "g_kv", "w_uk", "w_uv", "w_pool", "pool_scale", "w_o", "g_ffn", "w_up", "conv_w",
          "conv_b", "w_down", "g_final"]


def _laid_out(name, v):
    import numpy as np

    if name == "w_in":
        ends = [COL_Q + P * i for i in range(4)] + [COL_C] + [COL_QI + P * i for i in range(4)] + [COL_KI]
        ends += [COL_U + P * i for i in range(5)]
        tiles = [v[:, a:b].reshape(KT, P, b - a).transpose(1, 0, 2).reshape(P, -1) for a, b in zip(ends, ends[1:])]
        return np.concatenate(tiles, axis=1)
    if name in ("w_o", "w_up", "w_down"):
        k, n = v.shape
        return v.reshape(k // P, P, n // P, P).transpose(2, 1, 0, 3)
    if name in ("g_mix", "g_ffn", "pool_scale", "conv_b"):
        return v.reshape(-1, P).T
    if name == "conv_w":
        return v.reshape(CONV, -1, P).transpose(2, 0, 1)
    if name == "w_uk":
        return v.reshape(H // 2, P, CL).transpose(1, 0, 2)
    if name == "w_uv":
        return v.transpose(1, 0, 2)
    if name == "w_pool":
        return v.transpose(1, 0, 2)
    return v


def kernel(**inputs):
    import numpy as np
    import concourse.bacc as bacc
    from concourse.bass_utils import run_bass_kernel_spmd

    nc = bacc.Bacc("TRN2", target_bir_lowering=False, num_devices=1)
    arrays, a = {}, {}
    for name in _NAMES:
        v = np.ascontiguousarray(inputs[name])
        if name != "g_final":
            v = v.reshape(v.shape[1:])
        v = np.ascontiguousarray(_laid_out(name, v))
        arrays["in_" + name] = v
        a[name] = nc.dram_tensor("in_" + name, v.shape, mybir.dt.from_np(v.dtype), kind="ExternalInput").ap()
    y = nc.dram_tensor("y", (SEQ, DM), F32, kind="ExternalOutput").ap()
    w = {n: a[n] for n in ("w_in", "w_o", "w_up", "w_down")}
    program(nc, a["x"], y, w, a["g_mix"], a["g_kv"], a["w_uk"], a["w_uv"], a["w_pool"], a["pool_scale"], a["g_ffn"],
            a["conv_w"], a["conv_b"], a["g_final"])
    r = run_bass_kernel_spmd(nc, [arrays], core_ids=[0])
    return r.results[0]["y"].reshape(1, SEQ, DM)
```

```python
import concourse.bass as bass
from concourse import mybir
from contextlib import ExitStack

F32 = mybir.dt.float32
F32R = mybir.dt.float32r
U32 = mybir.dt.uint32
U8 = mybir.dt.uint8
I32 = mybir.dt.int32
I16 = mybir.dt.int16
ALU = mybir.AluOpType
ACT = mybir.ActivationFunctionType

P = 128
SEQ = 2048
DM = 1024
KT = DM // P
TB = 512
NBLK = SEQ // TB
JT = TB // P
NT = SEQ // P
H = 8
DH = 64
CL = 128
TOPK = 256
FF = 2816
NF = FF // P
FF_PARTS = [(0, 8), (8, 15), (15, NF)]
PART = max(b - a for a, b in FF_PARTS)
COL_Q, COL_C, COL_QI, COL_KI, COL_U = 0, 512, 640, 1152, 1224
KW = 72
WINDOWS = (2, 4, 8, 16)
HALO = 16
CHUNK = 1024
CONV = 3
EPS = 1e-6
BIG = 1e30
FLT_MAX = 3.4028234663852886e38
DIST_BASE = SEQ - P
NRING = 2
NLG = 4


def weight_units(w):
    def cols(name, a, n, k0=0, k1=KT):
        if name == "w_in":
            src = w[name][:, KT * a:KT * (a + n)].rearrange("p (k n) -> p k n", n=n)
        else:
            src = w[name][a // P]
        return src[:, k0:k1, :], k1 - k0, n

    def ffn():
        out = []
        for a, b in FF_PARTS:
            for i in range(a, b):
                out += [cols("w_up", i * P, P), cols("w_up", FF + i * P, P)]
            out += [cols("w_down", m * P, P, a, b) for m in range(KT)]
        return out

    units, at = [], {}
    for g in range(NBLK):
        at["in", g] = len(units)
        units += [cols("w_in", COL_C, CL), cols("w_in", COL_KI, KW)]
        for start in (COL_U, COL_QI, COL_Q):
            units += [cols("w_in", start + m * P, P) for m in range(4)]
        if g:
            at["ffn", g - 1] = len(units)
            units += ffn()
        at["o", g] = len(units)
        units += [cols("w_o", m * P, P) for m in range(KT)]
    at["ffn", NBLK - 1] = len(units)
    units += ffn()
    return units, at


def program(nc, x, y, w, g_mix, g_kv, w_uk, w_uv, w_pool, pool_scale, g_ffn, conv_w, conv_b, g_final):
    units, unit_at = weight_units(w)
    NU = len(units)

    ctx = ExitStack()
    with ctx:
        def sb(name, shape, dt, stack=None):
            return (stack or ctx).enter_context(nc.sbuf_tensor(name, shape, dt))

        def sem(name):
            return ctx.enter_context(nc.semaphore(name))

        wraw = sb("wraw", [P, NRING, KT, P], F32)
        wH, wL = sb("wH", [P, NRING, KT, P], F32R), sb("wL", [P, NRING, KT, P], F32R)
        ident = sb("ident", [P, P], F32)
        ones = sb("ones", [P, P], F32)
        dist = sb("dist", [P, SEQ], I16)
        ukH, ukL = sb("ukH", [P, H, CL], F32R), sb("ukL", [P, H, CL], F32R)
        uvH, uvL = sb("uvH", [P, H * DH], F32R), sb("uvL", [P, H * DH], F32R)
        wpH, wpL = sb("wpH", [P, 4, P], F32R), sb("wpL", [P, 4, P], F32R)
        gm, gf = sb("gm", [P, KT], F32), sb("gf", [P, KT], F32)
        psc = sb("psc", [P, 4], F32)
        gkv = sb("gkv", [P, CL], F32)
        cw = sb("cw", [P, 3, 2 * NF], F32)
        cb = sb("cb", [P, 2 * NF], F32)
        ahalo = sb("ahalo", [P, 2, 2 * NF, 2], F32)
        uhalo = sb("uhalo", [P, 4, HALO], F32)
        invc = sb("invc", [P, 4, HALO], F32)
        st = sb("st", [P, 24], F32)
        wabs, wsgn, wS = sb("wabs", [P, JT, H], F32), sb("wsgn", [P, JT, H], F32), sb("wS", [P, JT, H], F32)
        cand, drop, cnt = sb("cand", [P, 4], U32), sb("drop", [P, 4], U32), sb("cnt", [P, 4], F32)
        need = sb("need", [P, 2], F32)
        mx, nb = sb("mx", [P, 4, NBLK], F32), sb("nb", [P, 4], F32)
        lsum, rl = sb("lsum", [P, 2, 4, NBLK], F32), sb("rl", [P, 4], F32)

        def area(*layouts):
            made = []
            for layout in layouts:
                with ExitStack() as s:
                    made.append([sb(n, shape, dt, s) for n, shape, dt in layout])
            return made

        (kiH, kiL, cTH, cTL, cH, cL), (gH, gL, asb, acc, th), (xn2,), (yb,), \
            (_, counted0, eqm0, tiem0, rank0) = area(
            [("kiH", [P, SEQ], F32R), ("kiL", [P, SEQ], F32R), ("cTH", [P, SEQ], F32R), ("cTL", [P, SEQ], F32R),
             ("cH", [P, NT, CL], F32R), ("cL", [P, NT, CL], F32R)],
            [("gH", [P, PART, TB], F32R), ("gL", [P, PART, TB], F32R), ("asb", [P, 2, TB + 2], F32),
             ("acc", [P, 2, 2, TB], F32), ("th", [P, TB], F32)],
            [("xn2", [P, JT, DM], F32)],
            [("yb", [P, JT, DM], F32)],
            [("kiH0", [P, TB], F32), ("counted0", [P, JT, TB], U8), ("eqm0", [P, TB], U8), ("tiem0", [P, TB], U8),
             ("rank0", [P, TB], I16)])
        sb("key_area", [P, 6 * SEQ], F32)
        (actH, actL), (xr, xsq) = area([("actH", [P, KT, TB], F32R), ("actL", [P, KT, TB], F32R)],
                                       [("xr", [P, JT, DM], F32), ("xsq", [P, JT, DM], F32)])
        sb("act_area", [P, 2 * KT * TB], F32)
        (xb,), (qiS,), (prob,), (distI,) = area(
            [("xb", [P, JT, DM], F32)], [("qiS", [P, H, TB], F32R)], [("prob", [P, 2, SEQ], F32)],
            [("distI", [P, SEQ], I32)])
        sb("residual_area", [P, JT * DM], F32)
        (score,), (xa, xn), (uT, s0, s1, pH, pL) = area(
            [("score", [P, JT, SEQ], F32)],
            [("xa", [P, JT, DM], F32), ("xn", [P, JT, DM], F32)],
            [("uT", [P, 4, HALO + TB], F32), ("s0", [P, HALO + TB], F32), ("s1", [P, HALO + TB], F32),
             ("pH", [P, 4, TB], F32R), ("pL", [P, 4, TB], F32R)])
        sb("score_area", [P, JT * SEQ], F32)
        (qlH, qlL, pt, dgR, oH, oL), (poolF, qF, cF, cS, kwS), (_, counted, stage), (_, eqm, tiem, rank, gfin), \
            (ukR, ukS, uvS, wpS) = area(
            [("qlH", [P, 4, TB], F32R), ("qlL", [P, 4, TB], F32R),
             ("pt", [P, 2, 2, TB], F32R), ("dgR", [P, 4, P], F32), ("oH", [P, 4, P], F32R), ("oL", [P, 4, P], F32R)],
            [("poolF", [P, 4, TB], F32), ("qF", [P, 4, TB], F32), ("cF", [P, JT, CL], F32), ("cS", [P, TB], F32),
             ("kwS", [KW, TB], F32)],
            [("gap", [P, 8 * TB], F32), ("counted", [P, JT, SEQ], U8), ("stage", [P, 2, TB], F32)],
            [("gap2", [P, 8 * TB], F32), ("eqm", [P, SEQ], U8), ("tiem", [P, SEQ], U8), ("rank", [P, SEQ], I16),
             ("gfin", [P, DM], F32)],
            [("ukR", [P, 4, CL], F32), ("ukS", [P, H, CL], F32), ("uvS", [P, H * DH], F32), ("wpS", [P, 4, P], F32)])

        key_tiles = [kiH, kiL, cTH, cTL, cH, cL]
        key_store = [nc.dram_tensor(f"key_store{i}", [NBLK, P, TB], F32, kind="Internal").ap() for i in range(6)]
        x1_store = nc.dram_tensor("x1_store", [SEQ, DM], F32, kind="Internal").ap()

        def key_columns(i, b0, b1):
            t = f(key_tiles[i][:])
            t = t if i < 4 else t.rearrange("p t c -> p (t c)")
            return t[:, b0 * TB:b1 * TB].rearrange("p (b n) -> p b n", n=TB)

        ps = ctx.enter_context(nc.psum_tensor("ps", [P, 8, 512], F32))

        c_loaded = sem("c_loaded")
        c_made = sem("c_made")
        c_hi, c_lo, uk_scaled = sem("c_hi"), sem("c_lo"), sem("uk_scaled")
        w_loaded = [sem(f"w_loaded{i}") for i in range(NRING)]
        w_hi, w_lo, unit_done = sem("w_hi"), sem("w_lo"), sem("unit_done")
        x_loaded = [sem(f"x_loaded{j}") for j in range(JT)]
        gfin_loaded = sem("gfin_loaded")
        sq_done, var_ready, std_ready, xn_ready = sem("sq_done"), sem("var_ready"), sem("std_ready"), sem("xn_ready")
        csq_done = sem("csq_done")
        tr_full, tr_hi, tr_free = sem("tr_full"), sem("tr_hi"), sem("tr_free")
        pooled_full, pj_act, pj_dve, pj_hi = sem("pooled_full"), sem("pj_act"), sem("pj_dve"), sem("pj_hi")
        lg_full, lg_free, relu_done = sem("lg_full"), sem("lg_free"), sem("relu_done")
        lq_full, ttr_done, sums_copied = sem("lq_full"), sem("ttr_done"), sem("sums_copied")
        tok_ready, cF_hi = sem("tok_ready"), sem("cF_hi")
        pool_ready = sem("pool_ready")
        q_hi, q_lo = sem("q_hi"), sem("q_lo")
        d_ready = sem("d_ready")
        nb_ready, exp_done, pv_done = sem("nb_ready"), sem("exp_done"), sem("pv_done")
        o_free, dg_ready, o_hi, o_lo = sem("o_free"), sem("dg_ready"), sem("o_hi"), sem("o_lo")
        st_ready = sem("st_ready")
        rows_scaled = sem("rows_scaled")
        conv_in, taps_done, tanh_done, gu_ready, g_hi, g_lo = (sem("conv_in"), sem("taps_done"), sem("tanh_done"),
                                                              sem("gu_ready"), sem("g_hi"), sem("g_lo"))
        kv_made, kv_saved, ct_reloaded, ki_reloaded, c_reloaded = (sem("kv_made"), sem("kv_saved"), sem("ct_reloaded"),
                                                                  sem("ki_reloaded"), sem("c_reloaded"))
        x1_saved = sem("x1_saved")
        xr_loaded = [sem(f"xr_loaded{j}") for j in range(JT)]
        xr1_loaded = [sem(f"xr1_loaded{j}") for j in range(JT)]
        x1_loaded = [sem(f"x1_loaded{j}") for j in range(JT)]
        x1_ready, y_ready, y_stored = sem("x1_ready"), sem("y_ready"), sem("y_stored")
        dve_step, pool_step = sem("dve_step"), sem("pool_step")

        def f(ap):
            return ap.bitcast(F32)

        def rows(b, j):
            return slice(b * TB + j * P, b * TB + (j + 1) * P)

        def keys(t):
            return P * (t + 1)

        def chunks(t):
            return [(a, min(CHUNK, keys(t) - a)) for a in range(0, keys(t), CHUNK)]

        def quad(g, n, q):
            return 4 * q, min(4, JT * g + n // H + 1 - 4 * q)

        def prob_slots(g):
            slots = 2 * SEQ // (TB * (g + 1))
            return slots, min(3, slots - 1)

        def value_steps(g):
            Q, (_, ahead) = g + 1, prob_slots(g)
            NH = JT * H
            steps = [("query", h) for h in QUERY_ORDER[:4]] + [("outputs",)] + [("logits", n, q) for n in range(ahead) for q in range(Q)]
            steps += [("query", h) for h in QUERY_ORDER[4:]]
            last = None
            for n in range(NH):
                for q in range(Q):
                    m = n + ahead
                    if m < NH:
                        steps.append(("logits", m, q))
                    steps.append(("turn", n, q))
                    if last:
                        steps.append(("value",) + last)
                    last = (n, q)
                    if q == 0 and n % 4 == 0 and n:
                        steps.append(("recip", n // 4 - 1))
                    if q == 0 and n % 4 == 2 and n > 4:
                        steps.append(("norm", n // 4 - 1))
                if n % 4 == 1 and n > 4:
                    steps.append(("sums", n // 4 - 1))
                if n % 4 == 3 and n > 4:
                    steps.append(("out", n // 4 - 1))
            steps += [("value",) + last] + [(k, NH // 4 - 1) for k in ("recip", "sums", "norm", "out")]
            return steps

        QUERY_ORDER = (2, 3, 0, 1, 6, 7, 4, 5)
        act_slot = {0: 1, 1: 0, 4: 3, 5: 2}

        def latent_query(h, part):
            if h in act_slot:
                return (actH, actL)[part][:, act_slot[h], :]
            return (qlH, qlL)[part][:, h % 2 + 2 * (h // 4), :]

        def sums_after_o(g):
            return KT * (g + 1) + KT * len(FF_PARTS) * g

        def sums_after_ffn(b):
            return KT * (b + 1) + KT * len(FF_PARTS) * (b + 1)

        def o_banks(G):
            b = 2 if G % 2 == 0 else 6
            return ps[:, b:b + 2, :].rearrange("p b (h s n) -> p (b h) s n", h=2, s=2)

        def lg(k, n):
            b = 2 * (k % NLG)
            return ps[:, b:b + 2, :].rearrange("p b n -> p (b n)")[:, 0:n]

        def prob_row(g, n):
            slots, _ = prob_slots(g)
            w = TB * (g + 1)
            return prob[:].rearrange("p a b -> p (a b)")[:, (n % slots) * w:(n % slots + 1) * w]

        class Count:
            def __init__(self):
                self.n = 0

            def up(self, k=1):
                self.n += k
                return self.n

        len_ffn = 2 * NF + KT * len(FF_PARTS)
        block = ctx.enter_context(nc.Block())
        NCONST = 9

        @block.sync
        def _(sp):
            for j in range(JT):
                sp.dma_start(xa[:, j], x[rows(0, j)]).then_inc(x_loaded[j], 16)
            sp.dma_start(gm[:], g_mix).then_inc(c_loaded, 16)
            sp.dma_start(gf[:], g_ffn).then_inc(c_loaded, 16)
            sp.dma_start(psc[:], pool_scale).then_inc(c_loaded, 16)
            sp.dma_start(gkv[:], g_kv.rearrange("(a n) -> a n", a=1).to_broadcast([P, CL])).then_inc(c_loaded, 16)
            sp.dma_start(cw[:], conv_w).then_inc(c_loaded, 16)
            sp.dma_start(cb[:], conv_b).then_inc(c_loaded, 16)
            sp.dma_start(ukR[:], w_uk).then_inc(c_loaded, 16)
            sp.dma_start(uvS[:], w_uv.rearrange("p h d -> p (h d)")).then_inc(c_loaded, 16)
            sp.dma_start(wpS[:], w_pool).then_inc(c_loaded, 16)
            done = Count()

            def load_to(end):
                while done.n < min(end, NU):
                    u = done.n
                    src, kts, cols = units[u]
                    if u >= NRING:
                        sp.wait_ge(w_lo, u - NRING + 1)
                    sp.dma_start(wraw[:, u % NRING, 0:kts, 0:cols], src).then_inc(w_loaded[u % NRING], 16)
                    done.up()

            for g in range(NBLK):
                load_to(unit_at["in", g] + 14)
                sp.wait_ge(kv_made, g + 1)
                for i in range(6):
                    sp.dma_start(key_store[i][g:g + 1].rearrange("b p n -> p b n"), key_columns(i, g, g + 1)).then_inc(kv_saved, 16)
                if g:
                    def load_keys(i, loaded):
                        sp.dma_start(key_columns(i, 0, g + 1), key_store[i][0:g + 1].rearrange("b p n -> p b n")).then_inc(loaded, 16)

                    load_to(unit_at["ffn", g - 1] + len_ffn - KT + NRING)
                    sp.wait_ge(g_lo, NF * g)
                    load_keys(4, c_reloaded)
                    load_keys(5, c_reloaded)
                    load_to(unit_at["o", g] + NRING)
                    sp.wait_ge(unit_done, unit_at["ffn", g - 1] + len_ffn)
                    load_keys(2, ct_reloaded)
                    load_keys(3, ct_reloaded)
                    if g + 1 < NBLK:
                        sp.wait_ge(y_stored, 16 * JT * g)
                        load_keys(0, ki_reloaded)
                        load_keys(1, ki_reloaded)
                load_to(unit_at["o", g] + 2 * NRING)
                sp.wait_ge(o_lo, 2 * JT * (g + 1))
                for j in range(JT):
                    sp.dma_start(xb[:, j], x[rows(g, j)]).then_inc(xr_loaded[j], 16)
                if g + 1 < NBLK:
                    for j in range(JT):
                        sp.dma_start(xa[:, j], x[rows(g + 1, j)]).then_inc(x_loaded[j], 16)
            load_to(NU)

        @block.gpsimd
        def _(pool):
            step = Count()

            def link(ins):
                ins.then_inc(pool_step, 1)
                pool.wait_ge(pool_step, step.up())

            lows = Count()

            def weight_lows(end):
                while lows.n < min(end, NU):
                    u = lows.n
                    lows.up()
                    _, kts, cols = units[u]
                    s = u % NRING
                    pool.wait_ge(w_hi, u + 1)
                    if u >= NRING:
                        pool.wait_ge(unit_done, u - NRING + 1)
                    nc.gpsimd.tensor_tensor(wL[:, s, 0:kts, 0:cols], wraw[:, s, 0:kts, 0:cols],
                                            f(wH[:, s, 0:kts, 0:cols]), ALU.subtract).then_inc(w_lo, 1)

            link(nc.gpsimd.memset(ident[:], 0.0))
            link(nc.gpsimd.affine_select(out=ident[:], in_=ident[:], compare_op=ALU.not_equal, fill=1.0, base=0,
                                         pattern=[[-1, P]], channel_multiplier=1))
            nc.gpsimd.memset(ones[:], 1.0)
            nc.gpsimd.memset(uhalo[:], 0.0)
            nc.gpsimd.memset(ahalo[:], 0.0)
            for gi, win in enumerate(WINDOWS):
                for t in range(HALO):
                    nc.gpsimd.memset(invc[:, gi, t:t + 1], 1.0 / min(t + 1, win))
            nc.gpsimd.iota(distI[:], pattern=[[-1, SEQ]], base=DIST_BASE, channel_multiplier=1).then_inc(c_made, 1)
            def outputs(b):
                pool.wait_ge(unit_done, unit_at["ffn", b] + len_ffn)
                pool.wait_ge(x1_ready, sums_after_ffn(b))
                pool.dma_start(gfin[:], g_final.rearrange("(a n) -> a n", a=1).to_broadcast([P, DM])).then_inc(gfin_loaded, 16)
                for j in range(JT):
                    pool.wait_ge(y_ready, JT * b + j + 1)
                    pool.dma_start(y[rows(b, j)], yb[:, j]).then_inc(y_stored, 16)

            index_slots = 0
            for g in range(NBLK):
                weight_lows(unit_at["in", g] + 14 + NRING)
                index_slots += sum(H * len(chunks(JT * g + j)) for j in range(JT))
                if g:
                    pool.wait_ge(unit_done, unit_at["in", g] + 14)
                    pool.wait_ge(x1_saved, 16 * JT * g)
                    for j in range(JT):
                        pool.dma_start(xr[:, j], x1_store[rows(g - 1, j)]).then_inc(xr1_loaded[j], 16)
                    pool.wait_ge(lg_free, index_slots)
                    for j in range(JT):
                        pool.dma_start(xb[:, j], x1_store[rows(g - 1, j)]).then_inc(x1_loaded[j], 16)
                    weight_lows(unit_at["ffn", g - 1] + len_ffn - KT + NRING)
                for k in range(0, KT, 2):
                    pool.wait_ge(q_hi, 2 * g + 1 + k // 4)
                    src = qF[:, k:k + 2, :] if k < 4 else poolF[:, k - 4:k - 2, :]
                    nc.gpsimd.tensor_tensor(actL[:, k:k + 2, :], src, f(actH[:, k:k + 2, :]), ALU.subtract).then_inc(q_lo, 1)
                    if g:
                        weight_lows(lows.n + 1)
                if g:
                    weight_lows(unit_at["ffn", g - 1] + len_ffn + NRING)
                    outputs(g - 1)
                weight_lows(unit_at["o", g] + KT + NRING)
                if g + 1 < NBLK:
                    pool.wait_ge(x1_ready, sums_after_o(g))
                    for j in range(JT):
                        pool.dma_start(x1_store[rows(g, j)], xb[:, j]).then_inc(x1_saved, 16)
            weight_lows(NU)
            outputs(NBLK - 1)
            pool.wait_ge(y_stored, 16 * JT * NBLK)
            pool.wait_ge(kv_saved, 16 * 6 * NBLK)

        @block.tensor
        def _(pe):
            pj_kinds = []
            pj_release = {"act": pj_act, "dve": pj_dve, "stage": st_ready}
            tr_kinds = []
            tr_release = {"parts": tr_free, "residual": x1_ready, "sums": sums_copied}
            lgc, uc, lq, stc, turns = Count(), Count(), Count(), Count(), Count()

            def three(out, aH, aL, bH, bL, start, stop):
                nc.tensor.matmul(out, aL, bH, start=start, stop=False)
                nc.tensor.matmul(out, aH, bL, start=False, stop=False)
                return nc.tensor.matmul(out, aH, bH, start=False, stop=stop)

            def pj_slot(kind):
                k = len(pj_kinds)
                if k >= 4:
                    old = pj_kinds[k - 4]
                    n = pj_kinds[:k - 3].count(old)
                    pe.wait_ge(pj_release[old], n)
                pj_kinds.append(kind)
                return ps[:, k % 4]

            def pj_drained():
                for kind in pj_kinds[-4:]:
                    pe.wait_ge(pj_release[kind], pj_kinds.count(kind))

            def tr_slot(kind):
                k = len(tr_kinds)
                if k >= 2:
                    old = tr_kinds[k - 2]
                    pe.wait_ge(tr_release[old], tr_kinds[:k - 1].count(old))
                tr_kinds.append(kind)
                return ps[:, 4 + k % 2]

            def parts_made():
                pe.wait_ge(tr_free, tr_kinds.count("parts"))

            def next_unit():
                u = uc.n
                pe.wait_ge(w_lo, u + 1)
                uc.up()
                return u % NRING

            def down_pair(kts, gated):
                both = [(next_unit(), pj_slot("stage")) for _ in range(2)]
                for ks in (range(kts - 1), (kts - 1,)):
                    for s, out in both:
                        for k in ks:
                            pe.wait_ge(g_lo, gated + k + 1)
                            ins = three(out, wH[:, s, k, :], wL[:, s, k, :], gH[:, k, :], gL[:, k, :], k == 0, k == kts - 1)
                        if k == kts - 1:
                            ins.then_inc(unit_done, 1)

            def feature_unit(kind, rhsH, rhsL, kts):
                c = units[uc.n][2]
                s = next_unit()
                out = pj_slot(kind)[0:c]
                for k in range(kts):
                    ins = three(out, wH[:, s, k, 0:c], wL[:, s, k, 0:c], rhsH[:, k, :], rhsL[:, k, :], k == 0, k == kts - 1)
                ins.then_inc(unit_done, 1)

            def four_transposes(blocks):
                out = tr_slot("parts")
                for i, b in enumerate(blocks):
                    ins = nc.tensor.transpose(out[:, i * P:(i + 1) * P], b, ident[:])
                ins.then_inc(tr_full, 1)
                return ins

            norms = Count()

            def norm_transposes(src):
                pe.wait_ge(xn_ready, norms.up(JT))
                ready = []
                first, second = [(units[uc.n][2], next_unit(), pj_slot("act")) for _ in range(2)]

                def product(unit, k):
                    c, s, out = unit
                    pe.wait_ge(tr_free, ready[k])
                    ins = three(out[0:c], wH[:, s, k, 0:c], wL[:, s, k, 0:c], actH[:, k, :], actL[:, k, :], k == 0, k == KT - 1)
                    if k == KT - 1:
                        ins.then_inc(unit_done, 1)

                for k in range(KT + 2):
                    if k < KT:
                        four_transposes([src[:, j, k * P:(k + 1) * P] for j in range(JT)])
                        ready.append(tr_kinds.count("parts"))
                    if k >= 2:
                        product(first, k - 2)
                        if k - 2 < KT // 2:
                            product(second, k - 2)
                for k in range(KT // 2, KT):
                    product(second, k)

            def ffn(b):
                norm_transposes(xn2)
                for t0, t1 in FF_PARTS:
                    for i in range(max(t0, 1), t1):
                        feature_unit("act", actH, actL, KT)
                        feature_unit("act", actH, actL, KT)
                    down_pair(t1 - t0, NF * b + t0)
                    back_transposes(0)
                    for m in range(2, KT):
                        feature_unit("stage", gH, gL, t1 - t0)
                        back_transposes(m - 1)
                    back_transposes(KT - 1)

            def back_transposes(m):
                pe.wait_ge(st_ready, stc.up())
                out = tr_slot("residual")
                for j in range(JT):
                    ins = nc.tensor.transpose(out[:, j * P:(j + 1) * P], stage[:, m % 2, j * P:(j + 1) * P], ident[:])
                ins.then_inc(tr_full, 1)

            pe.wait_ge(c_made, 1)
            for g in range(NBLK):
                norm_transposes(xn)
                copied = pj_kinds.count("act")
                feature_unit("act", actH, actL, KT)
                pe.wait_ge(pj_act, copied)
                four_transposes([cS[:, j * P:(j + 1) * P] for j in range(JT)])
                out = tr_slot("parts")
                for j in range(JT):
                    ins = nc.tensor.transpose(out[:, j * KW:(j + 1) * KW], kwS[:, j * P:(j + 1) * P], ident[0:KW, 0:KW])
                ins.then_inc(tr_full, 1)
                for m in range(2):
                    feature_unit("act", actH, actL, KT)
                pe.wait_ge(tok_ready, g + 1)
                four_transposes([cF[:, j, :] for j in range(JT)])
                feature_unit("act", actH, actL, KT)
                for m in range(4):
                    feature_unit("dve", actH, actL, KT)
                for m in range(4):
                    feature_unit("act", actH, actL, KT)
                for m in range(4):
                    pe.wait_ge(pool_ready, 4 * g + m + 1)
                    out = pj_slot("act")
                    three(out, wpH[:, m, :], wpL[:, m, :], pH[:, m, :], pL[:, m, :], True, True).then_inc(pooled_full, 1)
                pj_drained()
                parts_made()
                if g > 1:
                    pe.wait_ge(ki_reloaded, 16 * 2 * (g - 1))
                for j in range(JT):
                    t = JT * g + j
                    for h in range(H):
                        for a, n in chunks(t):
                            k = lgc.n
                            if k >= NLG:
                                pe.wait_ge(lg_free, k - NLG + 1)
                            lgc.up()
                            out = lg(k, n)
                            for b in range(0, n, 512):
                                e = min(n, b + 512)
                                q = qiS[:, h, j * P:(j + 1) * P]
                                nc.tensor.matmul(out[:, b:e], q, kiL[:, a + b:a + e], start=True, stop=False)
                                ins = nc.tensor.matmul(out[:, b:e], q, kiH[:, a + b:a + e], start=False, stop=True)
                            ins.then_inc(lg_full, 1)

                pe.wait_ge(lg_free, lgc.n)
                if g:
                    ffn(g - 1)
                    pj_drained()
                made = {}

                def query(h):
                    three(tr_slot("parts"), ukH[:, h, :], ukL[:, h, :], actH[:, h // 2, :], actL[:, h // 2, :],
                          True, True).then_inc(tr_full, 1)
                    made[("query", h)] = tr_kinds.count("parts")

                def logits(n, q):
                    j, h = divmod(n, H)
                    if j == 0 and q == 0:
                        pe.wait_ge(tr_free, made[("query", h)])
                    k = lq.n
                    if k >= 2:
                        pe.wait_ge(ttr_done, k - 1)
                    a, m = quad(g, n, q)
                    keys_ = slice(a * P, (a + m) * P)
                    qH, qL = [latent_query(h, part)[:, j * P:(j + 1) * P] for part in range(2)]
                    three(ps[:, k % 2, 0:m * P], qH, qL, cTH[:, keys_], cTL[:, keys_],
                          True, True).then_inc(lq_full, 1)
                    lq.up()

                def turn(n, q):
                    pe.wait_ge(exp_done, turns.up())
                    a, m = quad(g, n, q)
                    out = tr_slot("parts")
                    pr = prob_row(g, n)
                    for i in range(m):
                        ins = nc.tensor.transpose(out[:, i * P:(i + 1) * P], pr[:, (a + i) * P:(a + i + 1) * P], ident[:])
                    ins.then_inc(tr_full, 1)
                    made[(n, q)] = (tr_kinds.count("parts"), turns.n - 1)

                def value(n, q):
                    j, h = divmod(n, H)
                    G = 8 * g + n // 4
                    if n % 4 == 0 and q == 0 and G >= 2:
                        pe.wait_ge(o_free, G - 1)
                    count, k = made[(n, q)]
                    pe.wait_ge(tr_free, count)
                    a, m = quad(g, n, q)
                    b = k % 2
                    out = o_banks(G)[:, h % 4]
                    for i in range(m):
                        both = pt[:, b, :, i * P:(i + 1) * P]
                        nc.tensor.matmul(out, cL[:, a + i, :], both, start=(a + i == 0), stop=False)
                        ins = nc.tensor.matmul(out, cH[:, a + i, :], both, start=False, stop=(a + i == JT * g + j))
                    ins.then_inc(pv_done, 1)

                def sums(G):
                    pe.wait_ge(dg_ready, 8 * g + G + 1)
                    nc.tensor.matmul(tr_slot("sums"), ones[:], dgR[:].rearrange("p a b -> p (a b)"),
                                     start=True, stop=True).then_inc(tr_full, 1)

                def out_heads(G):
                    pe.wait_ge(o_lo, 8 * g + G + 1)
                    out = tr_slot("parts")
                    for pp in range(2):
                        c = (2 * (G % 2) + pp) * P
                        ins = three(out[:, pp * 256:pp * 256 + 256], uvH[:, c:c + P], uvL[:, c:c + P],
                                    oH[:, 2 * pp:2 * pp + 2, :].rearrange("p a b -> p (a b)"),
                                    oL[:, 2 * pp:2 * pp + 2, :].rearrange("p a b -> p (a b)"), True, True)
                    ins.then_inc(tr_full, 1)
                    made[("out", G)] = tr_kinds.count("parts")

                products = []

                def project(n):
                    for _ in range(n):
                        (s, out), k = products.pop(0)
                        ins = three(out, wH[:, s, k, :], wL[:, s, k, :], actH[:, k, :], actL[:, k, :], k == 4, k == 3)
                        if k == 3:
                            ins.then_inc(unit_done, 1)

                pe.wait_ge(q_lo, KT // 2 * (g + 1))
                if g:
                    pe.wait_ge(ct_reloaded, 16 * 2 * g)
                    pe.wait_ge(c_reloaded, 16 * 2 * g)
                do = {"query": query, "logits": logits, "turn": turn, "value": value, "sums": sums, "out": out_heads}
                G = 2 * JT - 1
                for kind, *at in value_steps(g):
                    if (kind, *at) == ("sums", G):
                        pe.wait_ge(ttr_done, lq.n)
                        pe.wait_ge(o_free, 8 * g + G)
                        pair = [(next_unit(), pj_slot("stage")) for _ in range(2)]
                        products += [(unit, k) for ks in ((4, 5, 6, 7), (0, 1), (2, 3)) for unit in pair for k in ks]
                        project(3)
                    if (kind, *at) == ("out", G):
                        project(5)
                    if kind in do:
                        do[kind](*at)
                pe.wait_ge(tr_free, made[("out", G - 1)])
                project(4)
                parts_made()
                project(4)

                back_transposes(0)
                for m in range(2, KT):
                    feature_unit("stage", actH, actL, KT)
                    back_transposes(m - 1)
                back_transposes(KT - 1)
            ffn(NBLK - 1)

        @block.scalar
        def _(act):
            hi, pj, tr, lgc, var, ptc, biases = Count(), Count(), Count(), Count(), Count(), Count(), Count()

            def weight_highs(upto):
                while hi.n < min(upto, NU):
                    u = hi.n
                    _, kts, cols = units[u]
                    s = u % NRING
                    act.wait_ge(w_loaded[s], 16 * (u // NRING + 1))
                    if u >= NRING:
                        act.wait_ge(unit_done, u - NRING + 1)
                    nc.scalar.activation(wH[:, s, 0:kts, 0:cols], wraw[:, s, 0:kts, 0:cols], ACT.Copy).then_inc(w_hi, 1)
                    hi.up()

            def pj_wait(u):
                act.wait_ge(unit_done, u + 1)
                weight_highs(u + 1 + NRING)
                k = pj.n
                pj.up()
                return ps[:, k % 4]

            def square_sums(src, junk, loaded=None, count=0):
                for j in range(JT):
                    if loaded:
                        act.wait_ge(loaded[j], 16 * count)
                    nc.scalar.activation(junk[:, j], src[:, j], ACT.Square, accum_out=st[:, j:j + 1]).then_inc(sq_done, 1)

            def root():
                act.wait_ge(var_ready, var.up())
                nc.scalar.activation(st[:, 8:12], st[:, 4:8], ACT.Sqrt).then_inc(std_ready, 1)

            def tr_high(dst, scale=None):
                act.wait_ge(tr_full, tr.n + 1)
                src = ps[:, 4 + tr.n % 2, 0:dst.shape[1]]
                tr.up()
                if scale is None:
                    nc.scalar.activation(dst, src, ACT.Copy).then_inc(tr_hi, 1)
                else:
                    nc.scalar.activation(dst, src, ACT.Copy, scale=scale).then_inc(tr_hi, 1)

            square_sums(xa, xn, x_loaded, 1)
            root()
            weight_highs(NRING)
            act.wait_ge(c_loaded, 16 * NCONST)
            act.wait_ge(uk_scaled, H)
            nc.scalar.activation(ukH[:], ukS[:], ACT.Copy).then_inc(c_hi, 1)
            nc.scalar.activation(uvH[:], uvS[:], ACT.Copy).then_inc(c_hi, 1)
            nc.scalar.activation(wpH[:], wpS[:], ACT.Copy).then_inc(c_hi, 1)
            act.wait_ge(c_lo, 1)

            def stages(first_unit, between=None):
                for m in range(KT):
                    if between and m == 3:
                        between()
                    bank = pj_wait(first_unit + m)
                    if m >= 2:
                        act.wait_ge(tr_full, tr.n + m - 1)
                    nc.scalar.activation(stage[:, m % 2, :], bank, ACT.Copy).then_inc(st_ready, 1)
                tr.up(KT)

            def query_highs():
                nc.scalar.activation(actH[:, 0:4, :], qF[:], ACT.Copy).then_inc(q_hi, 1)
                nc.scalar.activation(actH[:, 4:8, :], poolF[:], ACT.Copy).then_inc(q_hi, 1)

            def ffn(b):
                if b + 1 == NBLK:
                    act.wait_ge(x1_ready, sums_after_o(b))
                    act.wait_ge(y_stored, 16 * JT * b)
                    square_sums(xb, xn2)
                    root()
                else:
                    act.wait_ge(kv_saved, 16 * 6 * (b + 2))
                    act.wait_ge(rows_scaled, b + 1)
                    for j in range(JT):
                        nc.scalar.activation(xn2[:, j], xr[:, j], ACT.Copy, scale=st[:, 20 + j:21 + j]).then_inc(xn_ready, 1)
                for k in range(KT):
                    tr_high(actH[:, k, :], gf[:, k:k + 1])
                act.wait_ge(pj_act, 14 * min(b + 2, NBLK) + 2 * NF * b)
                u = unit_at["ffn", b]

                def conv_input(i, s, u):
                    c = i + s * NF
                    bank = pj_wait(u)
                    n = NF * b + i
                    if n:
                        act.wait_ge(taps_done, 2 * (n - 1) + s + 1)
                    if n >= 2:
                        act.wait_ge(g_lo, n - 1)
                    nc.scalar.activation(asb[:, s, 0:2], ahalo[:, b % 2, c, :], ACT.Copy)
                    nc.scalar.activation(asb[:, s, 2:], bank, ACT.Copy)
                    nc.scalar.activation(acc[:, n % 2, s, :], bank, ACT.Identity, bias=cb[:, c:c + 1],
                                         scale=cw[:, 2, c:c + 1]).then_inc(conv_in, 1)
                    nc.scalar.activation(ahalo[:, (b + 1) % 2, c, :], bank[:, TB - 2:TB], ACT.Copy).then_inc(pj_act, 1)

                def gate_tanh(i):
                    n = NF * b + i
                    act.wait_ge(taps_done, 2 * n + 1)
                    if n:
                        act.wait_ge(gu_ready, n)
                    nc.scalar.activation(th[:], acc[:, n % 2, 0, :], ACT.Tanh, scale=0.5).then_inc(tanh_done, 1)

                def gated_high(i, t0):
                    n = NF * b + i
                    act.wait_ge(gu_ready, n + 1)
                    nc.scalar.activation(gH[:, i - t0, :], acc[:, n % 2, 1, :], ACT.Copy).then_inc(g_hi, 1)

                for t0, t1 in FF_PARTS:
                    for i in range(t0, t1):
                        conv_input(i, 0, u)
                        if i > t0:
                            gate_tanh(i - 1)
                        conv_input(i, 1, u + 1)
                        if i > t0:
                            gated_high(i - 1, t0)
                        u += 2
                    gate_tanh(t1 - 1)
                    gated_high(t1 - 1, t0)
                    if t1 == NF and b + 1 < NBLK:
                        query_highs()
                    stages(u)
                    u += KT
                act.wait_ge(x1_ready, sums_after_ffn(b))
                square_sums(xb, yb)

            for g in range(NBLK):
                u0 = unit_at["in", g]
                for k in range(KT):
                    tr_high(actH[:, k, :], gm[:, k:k + 1])
                def pool_channels(m):
                    bank = pj_wait(u0 + 2 + m)
                    nc.scalar.activation(uT[:, m, HALO:], bank, ACT.Copy).then_inc(pj_act, 1)

                bank = pj_wait(u0)
                nc.scalar.activation(cS[:], bank, ACT.Copy).then_inc(pj_act, 1)
                bank = pj_wait(u0 + 1)
                for r in range(2):
                    nc.scalar.activation(kiH[r * DH:(r + 1) * DH, g * TB:(g + 1) * TB], bank[0:DH], ACT.Copy)
                nc.scalar.activation(kwS[:], bank[0:KW], ACT.Copy).then_inc(pj_act, 1)
                pool_channels(0)
                act.wait_ge(tr_full, tr.n + 1)
                bank = ps[:, 4 + tr.n % 2]
                tr.up(2)
                for j in range(JT):
                    nc.scalar.activation(cF[:, j, :], bank[:, j * CL:(j + 1) * CL], ACT.Square,
                                         accum_out=st[:, j:j + 1]).then_inc(csq_done, 1)
                root()
                pool_channels(1)
                pool_channels(2)
                act.wait_ge(tok_ready, g + 1)
                tr_high(cTH[:, g * TB:(g + 1) * TB])
                nc.scalar.activation(cH[:, JT * g:JT * g + JT, :], cF[:], ACT.Copy).then_inc(cF_hi, 1)
                pool_channels(3)
                if g:
                    act.wait_ge(x1_saved, 16 * JT * g)
                for m in range(4):
                    bank = pj_wait(u0 + 6 + m)
                    nc.scalar.activation(qiS[0:64, 2 * m, :], bank[0:64], ACT.Copy).then_inc(pj_hi, 1)
                    nc.scalar.activation(qiS[0:64, 2 * m + 1, :], bank[64:128], ACT.Copy).then_inc(pj_hi, 1)
                for m in range(4):
                    bank = pj_wait(u0 + 10 + m)
                    nc.scalar.activation(qF[:, m, :], bank, ACT.Copy).then_inc(pj_act, 1)
                for m in range(4):
                    act.wait_ge(pooled_full, 4 * g + m + 1)
                    bank = ps[:, pj.n % 4]
                    pj.up()
                    nc.scalar.activation(poolF[:, m, :], bank, ACT.Copy, scale=psc[:, m:m + 1]).then_inc(pj_act, 1)
                for j in range(JT):
                    t = JT * g + j
                    for h in range(H):
                        for a, n in chunks(t):
                            act.wait_ge(lg_full, lgc.n + 1)
                            s = lg(lgc.n, n)
                            lgc.up()
                            nc.scalar.activation(s, s, ACT.Relu, scale=wabs[:, j, h:h + 1]).then_inc(relu_done, 1)
                    if g and j == 2:
                        square_sums(xr, xsq, xr1_loaded, g)
                        root()

                if g:
                    ffn(g - 1)
                else:
                    query_highs()
                Q = g + 1

                def exponentials(n, q):
                    if q == 0:
                        act.wait_ge(nb_ready, biases.up())
                    a, m = quad(g, n, q)
                    pr = prob_row(g, n)[:, a * P:(a + m) * P]
                    h = n % H
                    nc.scalar.activation(pr, pr, ACT.Exp, bias=nb[:, n % 4:n % 4 + 1], scale=2.0 ** -(h + 1),
                                         accum_out=lsum[:, (n // 4) % 2, n % 4, q:q + 1]).then_inc(exp_done, 1)

                def query(h):
                    tr_high(latent_query(h, 0))

                def turn(n, q):
                    if ptc.n >= 2:
                        act.wait_ge(pv_done, ptc.n - 1)
                    _, m = quad(g, n, q)
                    tr_high(pt[:, ptc.n % 2, 0, 0:m * P])
                    ptc.up()
                    if q + 1 < Q:
                        exponentials(n, q + 1)
                    elif n + 1 < JT * H:
                        exponentials(n + 1, 0)

                def sums(G):
                    act.wait_ge(tr_full, tr.n + 1)
                    src = ps[:, 4 + tr.n % 2]
                    tr.up()
                    nc.scalar.activation(dgR[:].rearrange("p a b -> p (a b)"), src, ACT.Copy).then_inc(sums_copied, 1)

                def norm(G):
                    act.wait_ge(o_free, 8 * g + G + 1)
                    nc.scalar.activation(oH[:], dgR[:], ACT.Copy).then_inc(o_hi, 1)

                def out_heads(G):
                    act.wait_ge(tr_full, tr.n + 1)
                    j, hg = divmod(G, 2)
                    for r in range(2):
                        rows = slice(64 * r, 64 * r + 64)
                        src = ps[rows, 4 + tr.n % 2].rearrange("p (a b) -> p a b", a=2)[:, :, r * P:(r + 1) * P]
                        ins = nc.scalar.activation(actH[rows, 2 * hg:2 * hg + 2, j * P:(j + 1) * P], src, ACT.Copy)
                    ins.then_inc(tr_hi, 1)
                    tr.up()

                def outputs():
                    if g:
                        root()

                do = {"query": query, "outputs": outputs, "turn": turn, "sums": sums, "norm": norm, "out": out_heads}
                first = True
                for kind, *at in value_steps(g):
                    if kind == "turn" and first:
                        exponentials(0, 0)
                        first = False
                    if kind in do:
                        do[kind](*at)

                def next_norm():
                    if g + 1 < NBLK:
                        square_sums(xa, xn, x_loaded, g + 2)
                        root()

                stages(unit_at["o", g], next_norm)
            ffn(NBLK - 1)
            root()

        @block.vector
        def _(dve):
            step, pj, tr, tr_parts, trh, lgc, relu, pjh, sqc, stdc, ptq, lq = [Count() for _ in range(12)]

            def link(ins):
                ins.then_inc(dve_step, 1)
                dve.wait_ge(dve_step, step.up())

            def rstd(width):
                nc.vector.tensor_scalar(st[:, 4:8], st[:, 0:4], 1.0 / width, EPS, ALU.mult, ALU.add).then_inc(var_ready, 1)
                dve.wait_ge(std_ready, stdc.up())
                link(nc.vector.reciprocal(st[:, 12:16], st[:, 8:12]))
                link(nc.vector.tensor_tensor(st[:, 16:20], st[:, 12:16], st[:, 12:16], ALU.mult))
                link(nc.vector.tensor_tensor(st[:, 16:20], st[:, 16:20], st[:, 4:8], ALU.mult))
                link(nc.vector.tensor_scalar(st[:, 16:20], st[:, 16:20], -0.5, 1.5, ALU.mult, ALU.add))
                link(nc.vector.tensor_tensor(st[:, 12:16], st[:, 12:16], st[:, 16:20], ALU.mult))

            def tr_low(dst, dstH, scale=None):
                dve.wait_ge(tr_hi, trh.up())
                n = dst.shape[1]
                src = ps[:, 4 + tr.n % 2, 0:n]
                tr.up()
                tr_parts.up()
                if scale is None:
                    nc.vector.tensor_tensor(dst, src, f(dstH), ALU.subtract).then_inc(tr_free, 1)
                else:
                    nc.vector.scalar_tensor_tensor(dst, src, scale, f(dstH), ALU.mult, ALU.subtract).then_inc(tr_free, 1)

            def row_scales():
                dve.wait_ge(sq_done, JT * sqc.up())
                rstd(DM)

            def normed(dst, src):
                row_scales()
                for j in range(JT):
                    nc.vector.tensor_scalar(dst[:, j], src[:, j], st[:, 12 + j:13 + j], None, ALU.mult).then_inc(xn_ready, 1)

            def normed_lows(scales):
                for k in range(KT):
                    tr_low(actL[:, k, :], actH[:, k, :], scales[:, k:k + 1])

            dve.wait_ge(c_loaded, 16 * NCONST)
            normed(xn, xa)
            link(nc.vector.memset(ukS[:], 0.0))
            for h in range(H):
                rows = slice(64 * (h % 2), 64 * (h % 2) + 64)
                nc.vector.tensor_scalar(ukS[rows, h, :], ukR[rows, h // 2, :], DH ** -0.5 * 2.0 ** (h + 1), None,
                                        ALU.mult).then_inc(uk_scaled, 1)
            dve.wait_ge(uk_scaled, H)
            dve.wait_ge(c_hi, 3)
            link(nc.vector.tensor_tensor(ukL[:], ukS[:], f(ukH[:]), ALU.subtract))
            link(nc.vector.tensor_tensor(uvL[:], uvS[:], f(uvH[:]), ALU.subtract))
            nc.vector.tensor_tensor(wpL[:], wpS[:], f(wpH[:]), ALU.subtract).then_inc(c_lo, 1)
            dve.wait_ge(c_lo, 1)
            def count(g, j, thr, op=ALU.is_ge):
                n = keys(JT * g + j)
                nc.vector.tensor_scalar((counted if g else counted0)[:, j, 0:n], score[:, j, 0:n], thr, None, op, ALU.add,
                                        accum_out=cnt[:, j:j + 1]).then_inc(dve_step, 1)
                step.up()

            def search(g):
                tiles = [j for j in range(JT) if JT * g + j >= 2]
                a, b = tiles[0], JT
                for j in tiles:
                    count(g, j, 0.0)
                    yield
                dve.wait_ge(dve_step, step.n)
                link(nc.vector.tensor_scalar(drop[:, a:b].bitcast(I32), cnt[:, a:b], float(TOPK), -1.0, ALU.is_lt, ALU.mult))
                nc.vector.tensor_scalar(cand[:, a:b], drop[:, a:b], 1 << 30, None, ALU.bitwise_xor).then_inc(dve_step, 1)
                made = step.up()
                yield
                for bit in range(30, -1, -1):
                    dve.wait_ge(dve_step, made)
                    for j in tiles:
                        count(g, j, cand[:, j:j + 1].bitcast(F32))
                        counts = step.n
                        yield
                    dve.wait_ge(dve_step, counts)
                    nc.vector.tensor_scalar(drop[:, a:b].bitcast(I32), cnt[:, a:b], float(TOPK), float(1 << bit),
                                            ALU.is_lt, ALU.mult).then_inc(dve_step, 1)
                    dropped = step.up()
                    yield
                    dve.wait_ge(dve_step, dropped)
                    if bit:
                        ins = nc.vector.scalar_tensor_tensor(cand[:, a:b], cand[:, a:b], 1 << (bit - 1), drop[:, a:b],
                                                             ALU.bitwise_xor, ALU.bitwise_xor)
                    else:
                        ins = nc.vector.tensor_tensor(cand[:, a:b], cand[:, a:b], drop[:, a:b], ALU.bitwise_xor)
                    ins.then_inc(dve_step, 1)
                    made = step.up()
                    yield
                dve.wait_ge(dve_step, made)

            def mask(g):
                def then(ins):
                    ins.then_inc(dve_step, 1)
                    return step.up()

                for j in range(JT):
                    t = JT * g + j
                    if t < 2:
                        continue
                    n = keys(t)
                    o = DIST_BASE - P * t
                    v = cand[:, j:j + 1].bitcast(F32)
                    sc, eq, tie, rk = score[:, j, 0:n], *[a[:, 0:n] for a in ((eqm, tiem, rank) if g else (eqm0, tiem0, rank0))]
                    if j:
                        dve.wait_ge(d_ready, JT * g + j)
                    then(nc.vector.tensor_scalar(tie, sc, v, None, ALU.is_gt, ALU.add, accum_out=need[:, 0:1]))
                    yield
                    made = then(nc.vector.tensor_scalar(eq, sc, v, None, ALU.is_equal))
                    yield
                    dve.wait_ge(dve_step, made)
                    then(nc.vector.tensor_scalar(need[:, 1:2], need[:, 0:1], -1.0, float(TOPK), ALU.mult, ALU.add))
                    made = then(nc.vector.tensor_tensor_scan(rk, eq, eq, 0.0, ALU.add, ALU.max))
                    yield
                    dve.wait_ge(dve_step, made)
                    made = then(nc.vector.scalar_tensor_tensor(tie, rk, need[:, 1:2], eq, ALU.is_le, ALU.mult))
                    yield
                    dve.wait_ge(dve_step, made)
                    made = then(nc.vector.scalar_tensor_tensor(eq, sc, v, tie, ALU.is_le, ALU.subtract))
                    yield
                    dve.wait_ge(dve_step, made)
                    nc.vector.scalar_tensor_tensor(sc, eq, BIG, dist[:, o:o + n], ALU.mult, ALU.max).then_inc(d_ready, 1)
                    yield

            def mask_all(j):
                n = keys(j)
                o = DIST_BASE - P * j
                link(nc.vector.tensor_copy(score[:, j, 0:n], dist[:, o:o + n]))
                nc.vector.memset(score[0:64, j, n - 64:n], BIG).then_inc(d_ready, 1)

            def threshold_and_mask(g):
                yield from search(g)
                yield from mask(g)

            def go_on(work, n):
                for _ in range(n):
                    next(work, None)

            def residual(work, n, alone=0, between=None):
                for m in range(KT):
                    if between and m == 2:
                        between()
                    dve.wait_ge(tr_full, tr.n + 1)
                    src = ps[:, 4 + tr.n % 2].rearrange("p (j c) -> p j c", j=JT)
                    tr.up()
                    dst = xb[:, :, m * P:(m + 1) * P]
                    nc.vector.tensor_tensor(dst, src, dst, ALU.add).then_inc(x1_ready, 1)
                    go_on(work, n + (m % 2) if m < KT - alone else 0)

            def ffn(b, work):
                if b + 1 == NBLK:
                    normed(xn2, xb)
                normed_lows(gf)
                go_on(work, 3)

                def taps(i, s, hurry):
                    n = NF * b + i
                    c = i + s * NF
                    dve.wait_ge(conv_in, 2 * n + s + 1)
                    d = acc[:, n % 2, s, :]
                    nc.vector.scalar_tensor_tensor(d, asb[:, s, 1:TB + 1], cw[:, 1, c:c + 1], d, ALU.mult,
                                                   ALU.add).then_inc(dve_step, 1)
                    tap = step.up()
                    go_on(work, 0 if hurry else 1)
                    dve.wait_ge(dve_step, tap)
                    nc.vector.scalar_tensor_tensor(d, asb[:, s, 0:TB], cw[:, 0, c:c + 1], d, ALU.mult,
                                                   ALU.add).then_inc(taps_done, 1)

                def gate(i, hurry):
                    n = NF * b + i
                    dve.wait_ge(tanh_done, n + 1)
                    dve.wait_ge(taps_done, 2 * n + 2)
                    nc.vector.scalar_tensor_tensor(th[:], th[:], 1.0, acc[:, n % 2, 0, :], ALU.add,
                                                   ALU.mult).then_inc(dve_step, 1)
                    opened = step.up()
                    go_on(work, 0 if hurry else 1)
                    dve.wait_ge(dve_step, opened)
                    nc.vector.scalar_tensor_tensor(acc[:, n % 2, 1, :], th[:], 0.5, acc[:, n % 2, 1, :], ALU.mult,
                                                   ALU.mult).then_inc(gu_ready, 1)

                def gate_low(i, t0):
                    n = NF * b + i
                    dve.wait_ge(g_hi, n + 1)
                    nc.vector.tensor_tensor(gL[:, i - t0, :], acc[:, n % 2, 1, :], f(gH[:, i - t0, :]),
                                            ALU.subtract).then_inc(g_lo, 1)

                for t0, t1 in FF_PARTS:
                    for i in range(t0, t1):
                        last = i == t1 - 1
                        taps(i, 0, last)
                        if i > t0:
                            gate(i - 1, last)
                        go_on(work, 0 if last else 1)
                        taps(i, 1, last)
                        if i > t0:
                            gate_low(i - 1, t0)
                        go_on(work, 0 if last else 2)
                    gate(t1 - 1, True)
                    gate_low(t1 - 1, t0)
                    go_on(work, 8)
                    if t0 == 0 and b + 1 < NBLK:
                        for j in range(JT):
                            dve.wait_ge(x1_loaded[j], 16 * (b + 1))
                    residual(work, 3, 2 if t1 == NF else 0)

            def outputs(b):
                row_scales()
                dve.wait_ge(gfin_loaded, 16 * (b + 1))
                for j in range(JT):
                    nc.vector.scalar_tensor_tensor(yb[:, j], xb[:, j], st[:, 12 + j:13 + j], gfin[:], ALU.mult,
                                                   ALU.mult).then_inc(y_ready, 1)

            for g in range(NBLK):
                normed_lows(gm)
                if g == 0:
                    dve.wait_ge(c_made, 1)
                    nc.vector.scalar_tensor_tensor(dist[:], distI[:], -1.0, distI[:], ALU.mult, ALU.max)
                tiles = slice(JT * g, JT * (g + 1))
                block_keys = slice(g * TB, (g + 1) * TB)
                dve.wait_ge(pj_act, 14 * g + 2 * NF * max(g - 1, 0) + 2)
                for r in range(2):
                    rows = slice(r * DH, (r + 1) * DH)
                    nc.vector.tensor_tensor(kiL[rows, block_keys], kwS[0:DH, :], f(kiH[rows, block_keys]), ALU.subtract)
                link(nc.vector.tensor_copy(uT[:, :, 0:HALO], uhalo[:]))
                dve.wait_ge(csq_done, 4 * (g + 1))
                rstd(CL)
                bank = ps[:, 4 + tr.n % 2]
                for j in range(JT):
                    ins = nc.vector.scalar_tensor_tensor(cF[:, j, :], bank[:, j * CL:(j + 1) * CL], st[:, 12 + j:13 + j],
                                                         gkv[:], ALU.mult, ALU.mult)
                ins.then_inc(tr_free, 1)
                tr.up()
                dve.wait_ge(tr_full, tr.n + 1)
                bank = ps[:, 4 + tr.n % 2, 0:JT * KW].rearrange("p (j n) -> p j n", n=KW)[:, :, DH:KW]
                link(nc.vector.tensor_scalar(wS[:], bank, H ** -0.5 * DH ** -0.5, None, ALU.mult))
                nc.vector.tensor_scalar(wsgn[:], wS[:], 0.0, 2.0, ALU.is_ge, ALU.mult).then_inc(tr_free, 1)
                tr.up()
                dve.wait_ge(tr_free, tr_parts.up(2))
                link(nc.vector.tensor_scalar(wsgn[:], wsgn[:], -1.0, None, ALU.add))
                nc.vector.tensor_tensor(wabs[:], wS[:], wsgn[:], ALU.mult).then_inc(tok_ready, 1)

                def pooling(m, win):
                    dve.wait_ge(pj_act, 14 * g + 2 * NF * max(g - 1, 0) + 2 + m + 1)
                    src, free, lo = uT[:, m, :], [s0[:], s1[:]], 0
                    for sh in [d for d in (1, 2, 4, 8) if d < win]:
                        lo += sh
                        link(nc.vector.tensor_tensor(free[0][:, lo:], src[:, lo:], src[:, lo - sh:HALO + TB - sh], ALU.add))
                        src, free = free[0], free[::-1]
                    other = free[0]
                    link(nc.vector.scalar_tensor_tensor(other[:, HALO:], src[:, HALO:], 1.0 / win, uT[:, m, HALO:],
                                                        ALU.mult, ALU.subtract))
                    if g == 0:
                        e = HALO + HALO
                        link(nc.vector.tensor_tensor(other[:, HALO:e], src[:, HALO:e], invc[:, m, :], ALU.mult))
                        link(nc.vector.tensor_tensor(other[:, HALO:e], other[:, HALO:e], uT[:, m, HALO:e], ALU.subtract))
                    link(nc.vector.tensor_copy(pH[:, m, :], other[:, HALO:]))
                    nc.vector.tensor_tensor(pL[:, m, :], other[:, HALO:], f(pH[:, m, :]), ALU.subtract).then_inc(pool_ready, 1)
                    dve.wait_ge(pool_ready, 4 * g + m + 1)

                pj.up(6)
                for m, win in enumerate(WINDOWS):
                    pooling(m, win)
                    if m == 0:
                        tr_low(cTL[:, block_keys], cTH[:, block_keys])
                        dve.wait_ge(cF_hi, g + 1)
                        nc.vector.tensor_tensor(cL[:, tiles, :], cF[:], f(cH[:, tiles, :]), ALU.subtract).then_inc(kv_made, 1)
                    dve.wait_ge(pj_hi, pjh.up(2))
                    bank = ps[:, pj.n % 4]
                    pj.up()
                    nc.vector.tensor_tensor(qiS[64:128, 2 * m, :], bank[0:64], f(qiS[0:64, 2 * m, :]), ALU.subtract)
                    nc.vector.tensor_tensor(qiS[64:128, 2 * m + 1, :], bank[64:128], f(qiS[0:64, 2 * m + 1, :]),
                                            ALU.subtract).then_inc(pj_dve, 1)
                link(nc.vector.tensor_copy(uhalo[:], uT[:, :, TB:TB + HALO]))
                pj.up(8)
                for j in range(JT):
                    t = JT * g + j
                    for h in range(H):
                        nch = len(chunks(t))
                        for a, n in chunks(t):
                            dve.wait_ge(relu_done, relu.up())
                            s = lg(lgc.n, n)
                            lgc.up()
                            dst = score[:, j, a:a + n]
                            if h == 0:
                                nc.vector.tensor_scalar(dst, s, wsgn[:, j, 0:1], None, ALU.mult).then_inc(lg_free, 1)
                            else:
                                dve.wait_ge(lg_free, lgc.n - nch)
                                nc.vector.scalar_tensor_tensor(dst, s, wsgn[:, j, h:h + 1], dst, ALU.mult,
                                                               ALU.add).then_inc(lg_free, 1)
                    if g and j == 2:
                        row_scales()
                        nc.vector.tensor_copy(st[:, 20:24], st[:, 12:16]).then_inc(rows_scaled, 1)
                    if t >= 2:
                        dve.wait_ge(lg_free, lgc.n)
                        link(nc.vector.memset(score[0:64, j, keys(t) - 64:keys(t)], -FLT_MAX))
                work = threshold_and_mask(g)
                if g:
                    ffn(g - 1, work)
                    pj.up(len_ffn)
                    for _ in work:
                        pass
                else:
                    mask_all(0)
                    mask_all(1)

                Q = g + 1

                def query(h):
                    tr_low(latent_query(h, 1), latent_query(h, 0))

                def logits(n, q):
                    j, h = divmod(n, H)
                    a, m = quad(g, n, q)
                    if n % H == 0 and q == 0:
                        if g == 0 and j == 2:
                            for _ in work:
                                pass
                        dve.wait_ge(d_ready, JT * g + j + 1)
                    dve.wait_ge(lq_full, lq.n + 1)
                    s = n % 4
                    if q:
                        dve.wait_ge(ttr_done, lq.n)
                    nc.vector.tensor_tensor_reduce(prob_row(g, n)[:, a * P:(a + m) * P], ps[:, lq.n % 2, 0:m * P],
                                                   score[:, j, a * P:(a + m) * P], 1.0,
                                                   mx[:, s, q - 1:q] if q else -FLT_MAX, ALU.subtract, ALU.max,
                                                   mx[:, s, q:q + 1]).then_inc(ttr_done, 1)
                    lq.up()
                    if q == Q - 1:
                        dve.wait_ge(ttr_done, lq.n)
                        nc.vector.tensor_scalar(nb[:, s:s + 1], mx[:, s, q:q + 1], -(2.0 ** -(h + 1)), None,
                                                ALU.mult).then_inc(nb_ready, 1)

                def turn(n, q):
                    _, m = quad(g, n, q)
                    b = ptq.n % 2
                    tr_low(pt[:, b, 1, 0:m * P], pt[:, b, 0, 0:m * P])
                    ptq.up()

                def recip(G):
                    ls = lsum[:, G % 2, :, 0:Q]
                    if Q > 1:
                        link(nc.vector.tensor_reduce(rl[:], ls, mybir.AxisListType.X, ALU.add))
                        link(nc.vector.reciprocal(rl[:], rl[:]))
                    else:
                        link(nc.vector.reciprocal(rl[:], lsum[:, G % 2, :, 0]))
                    nc.vector.tensor_tensor(dgR[:], ident[:].unsqueeze(1).to_broadcast([P, 4, P]),
                                            rl[:].unsqueeze(2).to_broadcast([P, 4, P]), ALU.mult).then_inc(dg_ready, 1)

                def sums(G):
                    dve.wait_ge(sums_copied, 8 * g + G + 1)
                    tr.up()
                    dve.wait_ge(pv_done, valued[G])
                    o = o_banks(8 * g + G)
                    link(nc.vector.tensor_tensor(o[:, :, 1, :], o[:, :, 1, :], dgR[:], ALU.mult))
                    link(nc.vector.tensor_tensor(dgR[:], o[:, :, 0, :], dgR[:], ALU.mult))
                    nc.vector.tensor_tensor(dgR[:], o[:, :, 1, :], dgR[:], ALU.add).then_inc(o_free, 1)

                def norm(G):
                    dve.wait_ge(o_hi, 8 * g + G + 1)
                    nc.vector.tensor_tensor(oL[:], dgR[:], f(oH[:]), ALU.subtract).then_inc(o_lo, 1)

                def out_heads(G):
                    j, hg = divmod(G, 2)
                    dve.wait_ge(tr_hi, trh.up())
                    for r in range(2):
                        rows = slice(64 * r, 64 * r + 64)
                        src = ps[rows, 4 + tr.n % 2].rearrange("p (a b) -> p a b", a=2)[:, :, r * P:(r + 1) * P]
                        ins = nc.vector.tensor_tensor(actL[rows, 2 * hg:2 * hg + 2, j * P:(j + 1) * P], src,
                                                      f(actH[rows, 2 * hg:2 * hg + 2, j * P:(j + 1) * P]), ALU.subtract)
                    ins.then_inc(tr_free, 1)
                    tr.up()
                    tr_parts.up()

                valued = [ptq.n + 4 * Q * (G + 1) for G in range(2 * JT)]
                def last_outputs():
                    if g:
                        outputs(g - 1)
                        dve.wait_ge(y_ready, JT * g)

                do = {"query": query, "outputs": last_outputs, "logits": logits, "turn": turn, "recip": recip,
                      "sums": sums, "norm": norm, "out": out_heads}
                for kind, *at in value_steps(g):
                    if kind in do:
                        do[kind](*at)
                        if g == 0:
                            go_on(work, 3)

                def next_norm():
                    if g + 1 < NBLK:
                        normed(xn, xa)

                for j in range(JT):
                    dve.wait_ge(xr_loaded[j], 16 * (g + 1))
                residual(iter(()), 0, between=next_norm)
                pj.up(KT)
            ffn(NBLK - 1, iter(()))
            outputs(NBLK - 1)


_NAMES = ["x", "g_mix", "w_in", "g_kv", "w_uk", "w_uv", "w_pool", "pool_scale", "w_o", "g_ffn", "w_up", "conv_w",
          "conv_b", "w_down", "g_final"]


def _laid_out(name, v):
    import numpy as np

    if name == "w_in":
        ends = [COL_Q + P * i for i in range(4)] + [COL_C] + [COL_QI + P * i for i in range(4)] + [COL_KI]
        ends += [COL_U + P * i for i in range(5)]
        tiles = [v[:, a:b].reshape(KT, P, b - a).transpose(1, 0, 2).reshape(P, -1) for a, b in zip(ends, ends[1:])]
        return np.concatenate(tiles, axis=1)
    if name in ("w_o", "w_up", "w_down"):
        k, n = v.shape
        return v.reshape(k // P, P, n // P, P).transpose(2, 1, 0, 3)
    if name in ("g_mix", "g_ffn", "pool_scale", "conv_b"):
        return v.reshape(-1, P).T
    if name == "conv_w":
        return v.reshape(CONV, -1, P).transpose(2, 0, 1)
    if name == "w_uk":
        return v.reshape(H // 2, P, CL).transpose(1, 0, 2)
    if name == "w_uv":
        return v.transpose(1, 0, 2)
    if name == "w_pool":
        return v.transpose(1, 0, 2)
    return v


def kernel(**inputs):
    import numpy as np
    import concourse.bacc as bacc
    from concourse.bass_utils import run_bass_kernel_spmd

    nc = bacc.Bacc("TRN2", target_bir_lowering=False, num_devices=1)
    arrays, a = {}, {}
    for name in _NAMES:
        v = np.ascontiguousarray(inputs[name])
        if name != "g_final":
            v = v.reshape(v.shape[1:])
        v = np.ascontiguousarray(_laid_out(name, v))
        arrays["in_" + name] = v
        a[name] = nc.dram_tensor("in_" + name, v.shape, mybir.dt.from_np(v.dtype), kind="ExternalInput").ap()
    y = nc.dram_tensor("y", (SEQ, DM), F32, kind="ExternalOutput").ap()
    w = {n: a[n] for n in ("w_in", "w_o", "w_up", "w_down")}
    program(nc, a["x"], y, w, a["g_mix"], a["g_kv"], a["w_uk"], a["w_uv"], a["w_pool"], a["pool_scale"], a["g_ffn"],
            a["conv_w"], a["conv_b"], a["g_final"])
    r = run_bass_kernel_spmd(nc, [arrays], core_ids=[0])
    return r.results[0]["y"].reshape(1, SEQ, DM)
```
